# Optimizing a Trainium2 kernel written in Bass

```python
import math
import jax
import jax.numpy as jnp
from jax import lax
import numpy as np

D_MODEL = 2048
BATCH = 1
SEQ = 256
DEPTH = 2

N_HEADS = 16
HEAD_DIM = D_MODEL // N_HEADS
BRANCH = N_HEADS * HEAD_DIM
PLE_DIM = 256
ROPE_THETA = 10000.0
SB_Q_BLOCK = 128
MOBA_BLOCK = 256
MOBA_TOPK = 3
MOBA_Q_CHUNK = 64
N_A = DEPTH // 2
N_B = DEPTH - N_A
DEEPNORM_ALPHA = (2.0 * DEPTH) ** 0.25
DEEPNORM_BETA = (8.0 * DEPTH) ** -0.25
LN_EPS = 1e-5
NEG_BIG = -1e30

kernel_name = 'yoco_stickbreak_moba_hybrid'

def layer_norm(x, g, b):
    xf = x.astype(jnp.float32)
    mu = jnp.mean(xf, axis=-1, keepdims=True)
    var = jnp.mean(jnp.square(xf - mu), axis=-1, keepdims=True)
    return ((xf - mu) * lax.rsqrt(var + LN_EPS)).astype(x.dtype) * g + b

def split_heads(t):
    b, s, _ = t.shape
    return t.reshape(b, s, N_HEADS, HEAD_DIM).transpose(0, 2, 1, 3)

def merge_heads(t):
    b, h, s, d = t.shape
    return t.transpose(0, 2, 1, 3).reshape(b, s, h * d)

def rope(t, pos):
    half = HEAD_DIM // 2
    inv_freq = ROPE_THETA ** (-jnp.arange(half, dtype=jnp.float32) / half)
    ang = pos.astype(jnp.float32)[:, None] * inv_freq[None, :]
    cos = jnp.cos(ang).astype(t.dtype)
    sin = jnp.sin(ang).astype(t.dtype)
    t1, t2 = t[..., :half], t[..., half:]
    return jnp.concatenate([t1 * cos - t2 * sin, t2 * cos + t1 * sin], axis=-1)

def stick_breaking_attention(q, k, v):
    b, h, s, dh = q.shape
    n_blk = s // SB_Q_BLOCK
    scale = 1.0 / math.sqrt(dh)
    qb = q.reshape(b, h, n_blk, SB_Q_BLOCK, dh).transpose(2, 0, 1, 3, 4)
    key_pos = jnp.arange(s)

    def block(args):
        qi, i = args
        t_idx = i * SB_Q_BLOCK + jnp.arange(SB_Q_BLOCK)
        z = jnp.einsum('bhqd,bhkd->bhqk', qi, k).astype(jnp.float32) * scale
        past = key_pos[None, :] < t_idx[:, None]
        log_beta = jax.nn.log_sigmoid(z)
        log_1m_beta = jnp.where(past, jax.nn.log_sigmoid(-z), 0.0)
        tail = lax.cumsum(log_1m_beta, axis=3, reverse=True) - log_1m_beta
        w = jnp.where(past, jnp.exp(log_beta + tail), 0.0)
        return jnp.einsum('bhqk,bhkd->bhqd', w.astype(v.dtype), v)

    out = lax.map(block, (qb, jnp.arange(n_blk)))
    return out.transpose(1, 2, 0, 3, 4).reshape(b, h, s, dh)

def moba_attention(q, k, v, k_mean):
    b, h, s, dh = q.shape
    sp = k.shape[2]
    nb = sp // MOBA_BLOCK
    k_top = min(MOBA_TOPK, nb)
    scale = 1.0 / math.sqrt(dh)
    qp = jnp.pad(q, ((0, 0), (0, 0), (0, sp - s), (0, 0)))
    kb = k.reshape(b, h, nb, MOBA_BLOCK, dh)
    vb = v.reshape(b, h, nb, MOBA_BLOCK, dh)
    n_chunks = sp // MOBA_Q_CHUNK
    qc = qp.reshape(b, h, n_chunks, MOBA_Q_CHUNK, dh).transpose(2, 0, 1, 3, 4)
    b_idx = jnp.arange(b)[:, None, None, None]
    h_idx = jnp.arange(h)[None, :, None, None]
    blk_ids = jnp.arange(nb)
    rank = jnp.arange(k_top)
    key_off = jnp.arange(MOBA_BLOCK)
    n_sel = k_top * MOBA_BLOCK

    def chunk(args):
        qi, c = args
        t_idx = c * MOBA_Q_CHUNK + jnp.arange(MOBA_Q_CHUNK)
        own = (c * MOBA_Q_CHUNK) // MOBA_BLOCK
        gate = jnp.einsum('bhqd,bhnd->bhqn', qi, k_mean).astype(jnp.float32)
        gate = jnp.where(blk_ids < own, gate, NEG_BIG)
        _, sel = lax.top_k(gate, k_top)
        sel_ok = rank < own
        k_sel = kb[b_idx, h_idx, sel]
        v_sel = vb[b_idx, h_idx, sel]
        s_sel = jnp.einsum('bhqd,bhqnld->bhqnl', qi, k_sel).astype(jnp.float32) * scale
        s_sel = jnp.where(sel_ok[:, None], s_sel, NEG_BIG)
        k_own = lax.dynamic_index_in_dim(kb, own, axis=2, keepdims=False)
        v_own = lax.dynamic_index_in_dim(vb, own, axis=2, keepdims=False)
        s_own = jnp.einsum('bhqd,bhld->bhql', qi, k_own).astype(jnp.float32) * scale
        own_pos = own * MOBA_BLOCK + key_off
        s_own = jnp.where(own_pos[None, :] <= t_idx[:, None], s_own, NEG_BIG)
        scores = jnp.concatenate([s_sel.reshape(b, h, MOBA_Q_CHUNK, n_sel), s_own], axis=-1)
        probs = jax.nn.softmax(scores, axis=-1).astype(v.dtype)
        p_sel = probs[..., :n_sel].reshape(b, h, MOBA_Q_CHUNK, k_top, MOBA_BLOCK)
        p_own = probs[..., n_sel:]
        return (jnp.einsum('bhqnl,bhqnld->bhqd', p_sel, v_sel)
                + jnp.einsum('bhql,bhld->bhqd', p_own, v_own))

    out = lax.map(chunk, (qc, jnp.arange(n_chunks)))
    out = out.transpose(1, 2, 0, 3, 4).reshape(b, h, sp, dh)
    return out[:, :, :s]

def stick_breaking_layer(x, w_in, w_out):
    q, k, v, z = jnp.split(x @ w_in, 4, axis=-1)
    o = stick_breaking_attention(split_heads(q), split_heads(k), split_heads(v))
    return (merge_heads(o) * jax.nn.silu(z)) @ w_out

def shared_kv(x, ln_g, ln_b, w_kv, pos):
    xs = layer_norm(x, ln_g, ln_b)
    k, v = jnp.split(xs @ w_kv, 2, axis=-1)
    k = rope(split_heads(k), pos)
    v = split_heads(v)
    s = x.shape[1]
    sp = -(-s // MOBA_BLOCK) * MOBA_BLOCK
    pad = ((0, 0), (0, 0), (0, sp - s), (0, 0))
    k = jnp.pad(k, pad)
    v = jnp.pad(v, pad)
    b, h, _, dh = k.shape
    k_mean = k.reshape(b, h, sp // MOBA_BLOCK, MOBA_BLOCK, dh).mean(axis=3)
    return k, v, k_mean

def moba_layer(x, w_in, w_out, k, v, k_mean, pos):
    q, z = jnp.split(x @ w_in, 2, axis=-1)
    o = moba_attention(rope(split_heads(q), pos), k, v, k_mean)
    return (merge_heads(o) * jax.nn.silu(z)) @ w_out

def setup_inputs(seed: int = 0) -> dict:
    key = jax.random.key(seed)
    ks = jax.random.split(key, 13)
    f32 = jnp.float32

    def nrm(k, shape, scale):
        return jax.random.normal(k, shape, f32) * scale

    return {
        'x': nrm(ks[0], (BATCH, SEQ, D_MODEL), 1.0),
        'p': nrm(ks[1], (DEPTH, BATCH, SEQ, PLE_DIM), 1.0),
        'w_in_a': nrm(ks[2], (N_A, D_MODEL, 4 * BRANCH), D_MODEL ** -0.5),
        'w_out_a': nrm(ks[3], (N_A, BRANCH, D_MODEL), BRANCH ** -0.5 * DEEPNORM_BETA),
        'w_kv': nrm(ks[4], (D_MODEL, 2 * BRANCH), D_MODEL ** -0.5),
        'ln_kv_g': 1.0 + nrm(ks[5], (D_MODEL,), 0.02),
        'ln_kv_b': nrm(ks[6], (D_MODEL,), 0.02),
        'w_in_b': nrm(ks[7], (N_B, D_MODEL, 2 * BRANCH), D_MODEL ** -0.5),
        'w_out_b': nrm(ks[8], (N_B, BRANCH, D_MODEL), BRANCH ** -0.5 * DEEPNORM_BETA),
        'ln_g': 1.0 + nrm(ks[9], (DEPTH, D_MODEL), 0.02),
        'ln_b': nrm(ks[10], (DEPTH, D_MODEL), 0.02),
        'w_ple': nrm(ks[11], (DEPTH, PLE_DIM, D_MODEL), PLE_DIM ** -0.5),
        'w_ple_gate': nrm(ks[12], (DEPTH, D_MODEL, D_MODEL), D_MODEL ** -0.5),
    }

def reference(x, p, w_in_a, w_out_a, w_kv, ln_kv_g, ln_kv_b, w_in_b, w_out_b,
              ln_g, ln_b, w_ple, w_ple_gate):
    pos = jnp.arange(x.shape[1], dtype=jnp.int32)
    k_sh = v_sh = km_sh = None
    for i in range(DEPTH):
        if i < N_A:
            y = stick_breaking_layer(x, w_in_a[i], w_out_a[i])
        else:
            if i == N_A:
                k_sh, v_sh, km_sh = shared_kv(x, ln_kv_g, ln_kv_b, w_kv, pos)
            y = moba_layer(x, w_in_b[i - N_A], w_out_b[i - N_A], k_sh, v_sh, km_sh, pos)
        x = layer_norm(DEEPNORM_ALPHA * x + y, ln_g[i], ln_b[i])
        x = x + (p[i] @ w_ple[i]) * jax.nn.sigmoid(x @ w_ple_gate[i])
    return x


_drawn_inputs = setup_inputs


def setup_inputs(seed=0):
    import zlib

    import numpy as np

    out = dict(_drawn_inputs(seed))
    spreads = {}
    factors = {'ln_kv_g': 8.0, 'ln_kv_b': 8.0}
    for name, (base, spread) in spreads.items():
        noise = np.random.default_rng([zlib.crc32(name.encode()), seed]).standard_normal(out[name].shape)
        drawn = base * np.exp(spread * noise) if base else spread * noise
        out[name] = jnp.asarray(drawn.astype(out[name].dtype))
    for name, factor in factors.items():
        out[name] = (out[name] * factor).astype(out[name].dtype)
    return out
```

```python
import math
from contextlib import ExitStack

import concourse.bass as bass
import numpy as np
from concourse import mybir

F32 = mybir.dt.float32
F32R = mybir.dt.float32r
BF16 = mybir.dt.bfloat16
ALU = mybir.AluOpType
ACT = mybir.ActivationFunctionType
AX = mybir.AxisListType

P = 128
NEG = -1e30
LN_EPS = 1e-5
COLS = 512
PIECE_K = 2
RAWS = 4
SPLITS = 8


def build(nc, xt, x, pt, w_in_a, w_out_a, w_kv, w_in_b, w_out_b, w_ple, w_ple_gate,
          ln_rows, ln_cols, rope, out):
    D, T = xt.shape
    TT = T // P
    KT = D // P
    DH = P
    HG = COLS // DH
    G = D // COLS
    PC = KT // PIECE_K
    HALF = DH // 2
    LAYERS = w_ple.shape[0]
    ALPHA = (2.0 * LAYERS) ** 0.25
    SCALE = 1.0 / math.sqrt(DH)
    SC = 3 * P
    assert TT == 2 and PC == SPLITS and LAYERS == 2 and HG == 4 and G == 4

    N_QKVZ = 0
    N_OUT = [N_QKVZ + 4 * G * PC, 0]
    N_PLE = [N_OUT[0] + G * PC, 0]
    N_GATE = [N_PLE[0] + G, 0]
    N_Q = N_GATE[0] + G * PC
    N_Z = N_Q + G * PC
    N_KV = N_Z + G * PC
    N_OUT[1] = N_KV + 2 * G * PC
    N_PLE[1] = N_OUT[1] + G * PC
    N_GATE[1] = N_PLE[1] + G
    PIECES = N_GATE[1] + G * PC
    C_QKVZ = 0
    C_OUT = [C_QKVZ + 4 * G, 0]
    C_GATE = [C_OUT[0] + G, 0]
    C_Q = C_GATE[0] + G
    C_Z = C_Q + G
    C_KV = C_Z + G
    C_OUT[1] = C_KV + 2 * G
    C_GATE[1] = C_OUT[1] + G
    S_X = 0
    S_OUT = [G, 5 * G]
    S_GATE = [2 * G, 6 * G]
    S_X2 = 3 * G
    S_KV = 4 * G
    FIRST_ROWS = PC - PIECE_K
    OUT_ORDER = ([(c, j) for c in (0, 1) for j in range(FIRST_ROWS)]
                 + [(c, j) for c in (0, 1) for j in range(FIRST_ROWS, PC)]
                 + [(c, j) for c in range(2, G) for j in range(PC)])

    with ExitStack() as ctx:
        def sb(name, shape, dt=F32):
            return ctx.enter_context(nc.sbuf_tensor(name, [P, *shape], dt))

        def sem(name):
            return ctx.enter_context(nc.semaphore(name))

        raw = sb("raw", [RAWS, PIECE_K, COLS])
        w_hi = sb("w_hi", [SPLITS, PIECE_K, COLS], F32R)
        w_lo = sb("w_lo", [SPLITS, PIECE_K, COLS], F32R)
        act0 = sb("act0", [2, KT, T], F32R)
        act1 = sb("act1", [2, KT, T], F32R)
        big0 = sb("big0", [TT * D])
        big1 = sb("big1", [TT * D])
        heads = sb("heads", [3 * HG * T + 2 * 2 * SC])
        v_or_z = sb("v_or_z", [TT, COLS])
        stage = sb("stage", [HG * T])
        ident = sb("ident", [P])
        neg_upper = sb("neg_upper", [P])
        neg_ones = sb("neg_ones", [P])
        past = sb("past", [P])
        ident16 = sb("ident16", [P], BF16)
        not_past = sb("not_past", [P], BF16)
        future = sb("future", [P], BF16)
        cos_sin = sb("cos_sin", [2, TT, HALF])
        ln_col = sb("ln_col", [3, 2, KT])
        stats = sb("stats", [TT, G, 6])
        moments = sb("moments", [TT, 2])
        var_eps = sb("var_eps", [TT])
        minus_half = sb("minus_half", [TT])
        rstd = sb("rstd", [TT])
        shift = sb("shift", [TT])
        neg_max = sb("neg_max", [2, 2 * TT])
        row_sum = sb("row_sum", [2, 2 * TT])
        acc = ctx.enter_context(nc.psum_tensor("acc", [P, 4 * COLS], F32))
        aux = ctx.enter_context(nc.psum_tensor("aux", [P, 4 * COLS], F32))
        x2_spill = nc.dram_tensor("x2_spill", [T, D], F32).ap()

        tokens = "p (t n) -> p t n"
        qn, kn, vn_a, zn_a = (big0[:, i * TT * COLS:(i + 1) * TT * COLS].rearrange(tokens, t=TT)
                              for i in range(4))
        q_all = big0[:, :].rearrange("p (h t) -> p h t", t=T)
        sz_all = big1[:, :].rearrange("p (h t) -> p h t", t=T)
        x_raw = big1[:, :].rearrange("p (k t) -> p k t", t=T)
        res = [big1[:, :].rearrange(tokens, t=TT), big0[:, :].rearrange(tokens, t=TT)]
        ple = [big0[:, :].rearrange(tokens, t=TT), big1[:, :].rearrange(tokens, t=TT)]
        HT = HG * T
        kT = heads[:, 0:HT].rearrange("p (h t) -> p h t", t=T)
        qT = heads[:, HT:2 * HT].rearrange("p (h t) -> p h t", t=T)
        prob = heads[:, 2 * HT:2 * HT + 4 * SC].rearrange("p (b h c) -> p b h c", b=2, c=SC)
        gt = heads[:, 2 * HT + 4 * SC:].rearrange("p (h t) -> p h t", t=T)
        gain = heads[:, 0:D]
        offset = heads[:, D:2 * D]
        rope_tmp = heads[:, 0:HT].rearrange("p (t h d) -> p t h d", t=TT, d=DH)
        roped_out = heads[:, 2 * HT:3 * HT].rearrange("p (t h d) -> p t h d", t=TT, d=DH)
        roped_rows = heads[:, 2 * HT:3 * HT].rearrange(tokens, t=TT)
        stage_kt = stage[:, :].rearrange("p (k t) -> p k t", t=T)
        stage_tn = stage[:, :].rearrange(tokens, t=TT)
        p_raw = stage[:, 0:PIECE_K * T].rearrange("p (k t) -> p k t", t=T)
        p_act = act0[:, :, KT - PIECE_K:KT, :]
        aux_b = aux[:, :].rearrange("p (b n) -> p b n", n=COLS)
        aux_kt = [aux[:, 0:HT].rearrange("p (k t) -> p k t", t=T),
                  aux[:, HT:2 * HT].rearrange("p (k t) -> p k t", t=T)]

        def acc_of(parity):
            if isinstance(parity, int):
                return acc[:, parity * 2 * COLS:(parity + 1) * 2 * COLS].rearrange(tokens, t=TT)
            return acc[:, bass.ts(parity, 2 * COLS)].rearrange(tokens, t=TT)

        def quarter(ap, c):
            return ap[:, HG * c:HG * c + HG] if isinstance(c, int) else ap[:, bass.ds(c * HG, HG)]

        def columns(ap, c):
            return ap[:, :, COLS * c:COLS * c + COLS] if isinstance(c, int) else ap[:, :, bass.ts(c, COLS)]

        def scores_of(b):
            return aux_b[:, 2 * b:2 * b + 2, 0:SC]

        w_landed = [sem(f"dma_w_landed{i}") for i in range(RAWS)]
        x_landed = [sem(f"dma_x_landed{i}") for i in range(G)]
        tables_landed = sem("dma_tables_landed")
        res_landed = [sem(f"dma_res_landed{i}") for i in range(G)]
        p_landed = sem("dma_p_landed")
        ln_rows_landed = sem("dma_ln_rows_landed")
        x2_spilled = sem("dma_x2_spilled")
        out_stored = sem("dma_out_stored")
        consts_done = sem("pool_consts_done")
        rstd_done = sem("pool_rstd_done")
        gained = sem("pool_gained")
        x1_ready = sem("pool_x1_ready")
        q_group_ready = sem("pool_q_group_ready")
        hi_ready = sem("act_hi_ready")
        act_hi = sem("act_operand_hi")
        p_hi = sem("act_p_hi")
        qT_ready = sem("act_qT_ready")
        kT_ready = sem("act_kT_ready")
        abs_done = sem("act_abs_done")
        exp_done = sem("act_exp_done")
        ln_done = sem("act_ln_done")
        probs_raw = sem("act_probs_raw")
        w_ready = sem("act_w_ready")
        sz_ready = sem("act_sz_ready")
        ple_evac = sem("act_ple_evac")
        sig_ready = sem("act_sig_ready")
        lo_ready = sem("dve_lo_ready")
        act_ready = sem("dve_operand_ready")
        p_ready = sem("dve_p_ready")
        chunk_evac = sem("dve_chunk_evac")
        sp_raw = sem("dve_sp_raw")
        sp_ready = sem("dve_sp_ready")
        gated = sem("dve_gated")
        rope_mul = sem("dve_rope_mul")
        roped = sem("dve_roped")
        neg_max_ready = sem("dve_neg_max_ready")
        inv_ready = sem("dve_inv_ready")
        probs_ready = sem("dve_probs_ready")
        stats_done = sem("dve_stats_done")
        moments_done = sem("dve_moments_done")
        var_done = sem("dve_var_done")
        shift_done = sem("dve_shift_done")
        normed = sem("dve_normed")
        full_ready = sem("dve_full_ready")
        x2_sum = sem("dve_x2_sum")
        x2_ready = sem("dve_x2_ready")
        piece_used = sem("pe_piece_used")
        qT_psum = sem("pe_qT_psum")
        kT_psum = sem("pe_kT_psum")
        scores_ready = sem("pe_scores_ready")
        cum_ready = sem("pe_cum_ready")
        probsT_psum = sem("pe_probsT_psum")
        pv_done = sem("pe_pv_done")
        zT_psum = sem("pe_zT_psum")
        lnT_psum = sem("pe_lnT_psum")
        x2T_psum = sem("pe_x2T_psum")

        block = ctx.enter_context(nc.Block())

        @block.sync
        def _(sp):
            def load(n, r, matrix, j, c):
                rows = matrix[j * PIECE_K * P:(j + 1) * PIECE_K * P, :]
                cols = rows[:, c * COLS:(c + 1) * COLS] if isinstance(c, int) else rows[:, bass.ts(c, COLS)]
                if not isinstance(n, int) or n >= RAWS:
                    sp.wait_ge(lo_ready, n - RAWS + 1)
                sp.dma_start(raw[:, r % RAWS], cols.rearrange("(k p) n -> p k n", p=P)) \
                    .then_inc(w_landed[r % RAWS], 16)

            def load_chunk(n, base, matrix, c):
                for j in range(PC):
                    load(n + j, (base + j) % SPLITS, matrix, j, c)

            wa = w_in_a[0]
            for c in range(G):
                sp.dma_start(x_raw[:, HG * c:HG * c + HG, :],
                             xt[c * COLS:(c + 1) * COLS, :].rearrange("(k p) t -> p k t", p=P)) \
                    .then_inc(x_landed[c], 16)
                if c < 2:
                    for j in (2 * c, 2 * c + 1):
                        load(j, j, wa, j, 0)
            for j in range(RAWS, PC):
                load(j, j, wa, j, 0)
            load_chunk(PC, 0, wa, G)
            with sp.Fori(0, G - 1) as g:
                n = g * (4 * PC) + 2 * PC
                load_chunk(n, 0, wa, g + 2 * G)
                load_chunk(n + PC, 0, wa, g + 3 * G)
                load_chunk(n + 2 * PC, 0, wa, g + 1)
                load_chunk(n + 3 * PC, 0, wa, g + 1 + G)
            load_chunk(N_OUT[0] - 2 * PC, 0, wa, 3 * G - 1)
            load_chunk(N_OUT[0] - PC, 0, wa, 4 * G - 1)

            def load_out_ple_gate(layer, w_out):
                n = N_OUT[layer]
                for i, (c, j) in enumerate(OUT_ORDER):
                    load(n + i, (n + i) % SPLITS, w_out, j, c)
                for c in range(G):
                    load(N_PLE[layer] + c, (N_PLE[layer] + c) % SPLITS, w_ple[layer], 0, c)
                with sp.Fori(0, G) as c:
                    load_chunk(c * PC + N_GATE[layer], N_GATE[layer], w_ple_gate[layer], c)

            load_out_ple_gate(0, w_out_a[0])
            with sp.Fori(0, 2 * G) as c:
                load_chunk(c * PC + N_Q, N_Q, w_in_b[0], c)
            with sp.Fori(0, G) as g:
                n = g * (2 * PC) + N_KV
                load_chunk(n, N_KV, w_kv, g)
                load_chunk(n + PC, N_KV, w_kv, g + G)
            load_out_ple_gate(1, w_out_b[0])
            with sp.Fori(0, G) as c:
                sp.wait_ge(x2_ready, c + (G + 1))
                sp.dma_start(out[:, bass.ts(c, COLS)].rearrange("(t p) n -> p t n", p=P),
                             columns(res[1], c)).then_inc(out_stored, 16)
            sp.wait_ge(out_stored, 16 * G)

        @block.gpsimd
        def _(pool):
            pool.dma_start(cos_sin[:, :, :, :], rope).then_inc(tables_landed, 16)
            pool.dma_start(ln_col[:, :, :, :], ln_cols).then_inc(tables_landed, 16)
            for ap, value in ((ident, 0.0), (neg_upper, -1.0), (neg_ones, -1.0), (past, 1.0),
                              (not_past, 0.0), (future, 0.0), (minus_half, -0.5)):
                nc.gpsimd.memset(ap[:, :], value).then_inc(consts_done, 1)
            pool.wait_ge(consts_done, 7)
            for ap, op, fill, step, mult in ((ident, ALU.not_equal, 1.0, -1, 1),
                                             (neg_upper, ALU.is_ge, 0.0, -1, 1),
                                             (past, ALU.is_gt, 0.0, 1, -1),
                                             (not_past, ALU.is_gt, NEG, 1, -1),
                                             (future, ALU.is_ge, NEG, -1, 1)):
                nc.gpsimd.affine_select(out=ap[:, :], in_=ap[:, :], compare_op=op, fill=fill, base=0,
                                        pattern=[[step, P]], channel_multiplier=mult) \
                    .then_inc(consts_done, 1)
            pool.wait_ge(consts_done, 8)
            nc.gpsimd.tensor_copy(ident16[:, :], ident[:, :]).then_inc(consts_done, 1)

            def load_res(layer, src):
                for c in range(G):
                    pool.dma_start(columns(res[layer], c),
                                   src[:, c * COLS:(c + 1) * COLS].rearrange("(t p) n -> p t n", p=P)) \
                        .then_inc(res_landed[c], 16)

            def load_p(layer):
                pool.dma_start(p_raw, pt[layer].rearrange("(k p) t -> p k t", p=P)).then_inc(p_landed, 16)

            def load_ln_rows(layer):
                for i, row in enumerate((gain, offset)):
                    pool.dma_start(row, ln_rows[layer, i:i + 1, :].broadcast_to((P, D))) \
                        .then_inc(ln_rows_landed, 16)

            def inverse_std(k):
                pool.wait_ge(var_done, k + 1)
                nc.gpsimd.tensor_tensor(rstd[:, :], var_eps[:, :], minus_half[:, :], ALU.pow) \
                    .then_inc(rstd_done, 1)

            def gain_and_offset(layer):
                pool.wait_ge(ln_rows_landed, 32 * (layer + 1))
                for c in range(G):
                    x1 = columns(res[layer], c)
                    row = lambda r: r[:, c * COLS:(c + 1) * COLS].unsqueeze(1).broadcast_to((P, TT, COLS))
                    pool.wait_ge(lnT_psum, (2 * G if layer else 0) + c + 1)
                    nc.gpsimd.tensor_tensor(x1, x1, row(gain), ALU.mult).then_inc(gained, 1)
                    pool.wait_ge(gained, layer * G + c + 1)
                    nc.gpsimd.tensor_tensor(x1, x1, row(offset), ALU.add).then_inc(x1_ready, 1)

            load_p(0)
            pool.wait_ge(act_ready, S_X + G)
            load_res(0, x)
            pool.wait_ge(act_ready, S_OUT[0] + G)
            load_ln_rows(0)
            inverse_std(0)
            gain_and_offset(0)
            with pool.Fori(0, G) as c:
                pool.wait_ge(x2_ready, c + 1)
                pool.dma_start(x2_spill[:, bass.ts(c, COLS)].rearrange("(t p) n -> p t n", p=P),
                               columns(res[0], c)).then_inc(x2_spilled, 16)
            inverse_std(1)
            with pool.Fori(0, G) as g:
                pool.wait_ge(qT_ready, g + (G + 1))
                pool.wait_ge(scores_ready, g * 2 + 2 * G)
                nc.gpsimd.tensor_copy(qT[:, :, :], quarter(q_all, g)).then_inc(q_group_ready, 1)
            pool.wait_ge(q_group_ready, G)
            pool.wait_ge(x2_spilled, 16 * G)
            load_res(1, x2_spill)
            pool.wait_ge(act_ready, S_KV + G)
            load_p(1)
            pool.wait_ge(act_ready, S_OUT[1] + G)
            load_ln_rows(1)
            inverse_std(2)
            gain_and_offset(1)

        @block.scalar
        def _(act):
            def split(n, r):
                act.wait_ge(w_landed[r % RAWS], n * 4 + (16 - 4 * (r % RAWS)))
                if not isinstance(n, int) or n >= SPLITS:
                    act.wait_ge(piece_used, n - SPLITS + 1)
                nc.scalar.activation(w_hi[:, r], raw[:, r % RAWS], ACT.Copy).then_inc(hi_ready, 1)

            def pieces(n, base, after=None, count=PC):
                for j in range(count):
                    if not isinstance(n, int) or n + j + SPLITS < PIECES:
                        split(n + (j + SPLITS), (base + j) % SPLITS)
                    for step in (after or {}).get(j, ()):
                        step()

            def operand_hi(k, dst, src, c):
                nc.scalar.activation(quarter(dst[:, 0], c), src, ACT.Copy).then_inc(act_hi, 1)

            def copy_qT(k, dst):
                act.wait_ge(qT_psum, k + 1)
                nc.scalar.activation(dst, aux_kt[0], ACT.Copy, scale=SCALE).then_inc(qT_ready, 1)

            def copy_kT(k):
                act.wait_ge(kT_psum, k + 1)
                nc.scalar.activation(kT, aux_kt[1], ACT.Copy).then_inc(kT_ready, 1)

            def exp_abs(k, b):
                act.wait_ge(scores_ready, k * 2 + (b + 1))
                nc.scalar.activation(prob[:, b], scores_of(b), ACT.Abs).then_inc(abs_done, 1)
                act.wait_ge(abs_done, k * 2 + (b + 1))
                nc.scalar.activation(prob[:, b], prob[:, b], ACT.Exp, scale=-1.0).then_inc(exp_done, 1)

            def log_1p(k):
                for b in range(2):
                    act.wait_ge(exp_done, k * 2 + (b + 1))
                    nc.scalar.activation(prob[:, b], prob[:, b], ACT.Ln, bias=1.0).then_inc(ln_done, 1)

            def stick_weights(k, b):
                act.wait_ge(cum_ready, k * 2 + (b + 1))
                nc.scalar.activation(prob[:, b], scores_of(b), ACT.Exp).then_inc(w_ready, 1)

            def silu_z(k, dst, src):
                act.wait_ge(zT_psum, k + 1)
                nc.scalar.activation(dst, src, ACT.Silu).then_inc(sz_ready, 1)

            def gated_hi(k, c, s):
                act.wait_ge(gated, k + 1)
                operand_hi(s, act1, gt, c)

            def silu_z_group(k):
                act.wait_ge(act_ready, k + G)
                silu_z(k, gt, aux[:, :].rearrange("p (b s n) -> p b s n", b=2, s=2)[:, :, 1])

            def softmax_exp(k, b):
                act.wait_ge(neg_max_ready, (k - G) * 2 + (b + 1))
                for t in range(TT):
                    for h in range(2):
                        lo, hi = (0, P) if t == 0 else (P, SC)
                        i = 2 * t + h
                        last = nc.scalar.activation(prob[:, b, h, lo:hi], aux_b[:, 2 * b + h, lo:hi], ACT.Exp,
                                                    bias=neg_max[:, b, i:i + 1],
                                                    accum_out=row_sum[:, b, i:i + 1])
                last.then_inc(probs_raw, 1)

            def copy_probsT(k, b):
                act.wait_ge(probsT_psum, (k - G) * 2 + (b + 1))
                nc.scalar.activation(prob[:, b], scores_of(b), ACT.Copy).then_inc(w_ready, 1)

            def x_hi(c):
                act.wait_ge(x_landed[c], 16)
                nc.scalar.activation(quarter(act0[:, 0], c), quarter(x_raw, c), ACT.Copy).then_inc(act_hi, 1)

            for c in range(G):
                x_hi(c)
                split(2 * c, 2 * c)
                split(2 * c + 1, 2 * c + 1)

            def after_k(k):
                return {2: [lambda: copy_qT(k, qT)]}

            def after_v(k):
                return {2: [lambda: copy_kT(k)], 4: [lambda: exp_abs(k, 0)],
                        5: [lambda: exp_abs(k, 1), lambda: log_1p(k)]}

            def after_z(k):
                return {2: [lambda: stick_weights(k, 0)], 3: [lambda: stick_weights(k, 1)]}

            def gate_group(k):
                return {2: [lambda: silu_z_group(k)], 3: [lambda: gated_hi(k, k, k)]}

            pieces(0, 0)
            pieces(PC, 0, after_k(0))
            with act.Fori(0, G - 1) as g:
                n = g * (4 * PC) + 2 * PC
                pieces(n, 0, after_v(g))
                pieces(n + PC, 0, after_z(g))
                pieces(n + 2 * PC, 0, gate_group(g))
                pieces(n + 3 * PC, 0, after_k(g + 1))
            pieces(N_OUT[0] - 2 * PC, 0, after_v(G - 1))
            pieces(N_OUT[0] - PC, 0, after_z(G - 1))

            def split_p(layer):
                act.wait_ge(p_landed, 16 * (layer + 1))
                act.wait_ge(piece_used, N_OUT[layer])
                nc.scalar.activation(p_act[:, 0], p_raw, ACT.Copy).then_inc(p_hi, 1)

            def ple_out(layer, c):
                act.wait_ge(piece_used, N_PLE[layer] + c + 1)
                src = (aux if c < 2 else acc)[:, (c % 2) * 2 * COLS:(c % 2 + 1) * 2 * COLS]
                nc.scalar.activation(columns(ple[layer], c), src.rearrange(tokens, t=TT), ACT.Copy) \
                    .then_inc(ple_evac, 1)

            def full_hi(k, c):
                act.wait_ge(full_ready, k + 1)
                operand_hi(k, act0, stage_kt, c)

            def sigmoid_gate(layer, c, parity):
                act.wait_ge(piece_used, c * PC + (N_GATE[layer] + PC))
                if not isinstance(c, int) or c + layer > 0:
                    act.wait_ge(x2_ready, c + layer * G)
                if layer == 0 and not isinstance(c, int):
                    act.wait_ge(x2T_psum, c)
                nc.scalar.activation(stage_tn, acc_of(parity), ACT.Sigmoid).then_inc(sig_ready, 1)

            def x2_hi(c):
                act.wait_ge(x2T_psum, c + 1)
                operand_hi(0, act1, aux_kt[0], c)

            def out_ple_gate(layer, after_out):
                n = N_OUT[layer]
                pieces(n, n, after_out | {12: [lambda: split_p(layer)]}, G * PC)
                n = N_PLE[layer]
                k = 2 * G * layer
                pieces(n, n, {c: [lambda c=c: ple_out(layer, c)] for c in range(G)}, G)
                n = N_GATE[layer]
                full_hi(k, 0)
                full_hi(k + 1, 1)
                pieces(n, n, {1: [lambda: full_hi(k + 2, 2)], 3: [lambda: full_hi(k + 3, 3)],
                              PC - 1: [lambda: sigmoid_gate(layer, 0, 0)]})
                with act.Fori(1, G - layer) as c:
                    pieces(c * PC + n, n, ({3: [lambda: x2_hi(c - 1)]} if layer == 0 else {})
                           | {PC - 1: [lambda: sigmoid_gate(layer, c, c % 2)]})
                if layer:
                    sigmoid_gate(layer, G - 1, (G - 1) % 2)

            out_ple_gate(0, gate_group(G - 1))

            def ln_hi(c):
                full_hi(c + G, c)

            pieces(N_Q, N_Q, {2: [lambda: x2_hi(G - 1)], 6: [lambda: ln_hi(0)]})
            with act.Fori(1, G) as c:
                pieces(c * PC + N_Q, N_Q, {2: [lambda: copy_qT(c + (G - 1), quarter(q_all, c - 1))],
                                           5: [lambda: ln_hi(c)]})
            pieces(N_Z, N_Z, {2: [lambda: copy_qT(2 * G - 1, quarter(q_all, G - 1))]})
            act.wait_ge(x2_spilled, 16 * G)
            with act.Fori(1, G) as c:
                pieces(c * PC + N_Z, N_Z,
                       {2: [lambda: silu_z(c + (G - 1), quarter(sz_all, c - 1), aux_kt[0])]})
            pieces(N_KV, N_KV, {2: [lambda: silu_z(2 * G - 1, quarter(sz_all, G - 1), aux_kt[0])]})

            def after_v_b(k):
                return {2: [lambda: copy_kT(k)], 4: [lambda: softmax_exp(k, 0)], 5: [lambda: softmax_exp(k, 1)]}

            def after_k_b(k):
                return {0: [lambda: copy_probsT(k, 0)], 1: [lambda: copy_probsT(k, 1)],
                        4: [lambda: gated_hi(k, k - G, k)]}

            with act.Fori(0, G - 1) as g:
                n = g * (2 * PC) + (N_KV + PC)
                pieces(n, N_KV, after_v_b(g + G))
                pieces(n + PC, N_KV, after_k_b(g + G))
            pieces(N_OUT[1] - PC, N_KV, after_v_b(2 * G - 1))
            out_ple_gate(1, after_k_b(2 * G - 1))

        @block.vector
        def _(dve):
            def split(n, r):
                dve.wait_ge(hi_ready, n + 1)
                nc.vector.tensor_tensor(w_lo[:, r], raw[:, r % RAWS], w_hi[:, r].bitcast(F32), ALU.subtract) \
                    .then_inc(lo_ready, 1)

            def pieces(n, base, after=None, count=PC):
                for j in range(count):
                    if not isinstance(n, int) or n + j + SPLITS < PIECES:
                        split(n + (j + SPLITS), (base + j) % SPLITS)
                    for step in (after or {}).get(j, ()):
                        step()

            def operand_lo(s, dst, src, c):
                dve.wait_ge(act_hi, s + 1)
                nc.vector.tensor_tensor(quarter(dst[:, 1], c), src, quarter(dst[:, 0], c).bitcast(F32),
                                        ALU.subtract).then_inc(act_ready, 1)

            def evacuate(n_end, parity, dst):
                dve.wait_ge(piece_used, n_end)
                nc.vector.tensor_scalar(dst, acc_of(parity), 1.0, None, ALU.mult).then_inc(chunk_evac, 1)

            def softplus(k, b):
                dve.wait_ge(ln_done, k * 2 + (b + 1))
                nc.vector.scalar_tensor_tensor(out=prob[:, b], in0=scores_of(b), scalar=0.0, in1=prob[:, b],
                                               op0=ALU.max, op1=ALU.add).then_inc(sp_raw, 1)
                dve.wait_ge(sp_raw, k * 2 + (b + 1))
                for h in range(2):
                    diagonal = prob[:, b, h].rearrange("p (s c) -> p s c", c=P)[:, 0:3:2]
                    last = nc.vector.tensor_tensor(diagonal, diagonal,
                                                   past[:, :].unsqueeze(1).broadcast_to((P, 2, P)), ALU.mult)
                last.then_inc(sp_ready, 1)

            def gate_group(k, c, sz):
                dve.wait_ge(sz_ready, k + 1)
                dve.wait_ge(pv_done, k * 2 + 2)
                o = aux[:, :].rearrange("p (b s n) -> p b s n", b=2, s=2)[:, :, 0]
                nc.vector.tensor_tensor(gt.rearrange("p (b h) t -> p b (h t)", b=2), o,
                                        sz.rearrange("p (b h) t -> p b (h t)", b=2), ALU.mult).then_inc(gated, 1)

            def gated_lo(k, c, s):
                operand_lo(s, act1, gt, c)

            for c in range(G):
                dve.wait_ge(act_hi, c + 1)
                nc.vector.tensor_tensor(quarter(act0[:, 1], c), quarter(x_raw, c),
                                        quarter(act0[:, 0], c).bitcast(F32), ALU.subtract).then_inc(act_ready, 1)
                split(2 * c, 2 * c)
                split(2 * c + 1, 2 * c + 1)

            def chunk_end(n, parity, dst):
                return {PC - 1: [lambda: evacuate(n + PC, parity, dst)]}

            def after_v(k):
                return {5: [lambda: softplus(k, 0)], 6: [lambda: softplus(k, 1)]}

            def gate_steps(k):
                return {2: [lambda: gate_group(k, k, gt)], 3: [lambda: gated_lo(k, k, k + G)]}

            dve.wait_ge(consts_done, 13)
            pieces(0, 0, chunk_end(0, 0, qn))
            pieces(PC, 0, chunk_end(PC, 1, kn))
            with dve.Fori(0, G - 1) as g:
                n = g * (4 * PC) + 2 * PC
                pieces(n, 0, after_v(g) | chunk_end(n, 0, vn_a))
                pieces(n + PC, 0, chunk_end(n + PC, 1, zn_a))
                pieces(n + 2 * PC, 0, gate_steps(g) | chunk_end(n + 2 * PC, 0, qn))
                pieces(n + 3 * PC, 0, chunk_end(n + 3 * PC, 1, kn))
            n = N_OUT[0] - 2 * PC
            pieces(n, 0, after_v(G - 1) | chunk_end(n, 0, vn_a))
            pieces(n + PC, 0, chunk_end(n + PC, 1, zn_a))

            def add_residual(layer, c, used):
                dve.wait_ge(piece_used, N_OUT[layer] + used)
                dve.wait_ge(res_landed[c], 16 * (layer + 1))
                r = columns(res[layer], c)
                nc.vector.scalar_tensor_tensor(out=r, in0=r, scalar=ALPHA, in1=acc_of(c % 2),
                                               op0=ALU.mult, op1=ALU.add).then_inc(chunk_evac, 1)
                dve.wait_ge(chunk_evac, C_OUT[layer] + c + 1)
                statistics(r, c)

            def statistics(r, c):
                for t in range(TT):
                    s = stats[:, t, c, :] if isinstance(c, int) else stats[:, t, bass.ds(c, 1), :]
                    last = nc.vector.bn_stats(s, r[:, t])
                last.then_inc(stats_done, 1)

            def find_shift(k):
                dve.wait_ge(stats_done, G * (k + 1))
                for t in range(TT):
                    last = nc.vector.bn_aggr(moments[:, t], stats[:, t])
                last.then_inc(moments_done, 1)
                dve.wait_ge(moments_done, k + 1)
                nc.vector.tensor_scalar(var_eps[:, :], moments[:, :, 1], LN_EPS, None, ALU.add).then_inc(var_done, 1)
                dve.wait_ge(rstd_done, k + 1)
                nc.vector.scalar_tensor_tensor(out=shift[:, :], in0=moments[:, :, 0], scalar=-1.0, in1=rstd[:, :],
                                               op0=ALU.mult, op1=ALU.mult).then_inc(shift_done, 1)
                dve.wait_ge(shift_done, k + 1)

            def normalise(src, dst):
                for t in range(TT):
                    last = nc.vector.tensor_scalar(dst[:, t], src[:, t], rstd[:, t:t + 1], shift[:, t:t + 1],
                                                   ALU.mult, ALU.add)
                last.then_inc(normed, 1)

            def full_quarter(k, c, pair, which, s):
                dve.wait_ge(lnT_psum, k + 1)
                dve.wait_ge(act_ready, s)
                for i in range(HG):
                    if isinstance(c, int):
                        g, b = (ln_col[:, which, s, HG * c + i:HG * c + i + 1] for s in range(2))
                    else:
                        g, b = (ln_col[:, which, s, bass.ds(c * HG + i, 1)] for s in range(2))
                    last = nc.vector.tensor_scalar(stage_kt[:, i], aux_kt[pair][:, i], g, b, ALU.mult, ALU.add)
                last.then_inc(full_ready, 1)

            def full_lo(s, c):
                operand_lo(s, act0, stage_kt, c)

            def split_p(layer):
                dve.wait_ge(p_hi, layer + 1)
                nc.vector.tensor_tensor(p_act[:, 1], p_raw, p_act[:, 0].bitcast(F32), ALU.subtract) \
                    .then_inc(p_ready, 1)

            def add_ple(layer, c):
                e = c + layer * G
                r = columns(res[layer], c)
                dve.wait_ge(sig_ready, e + 1)
                dve.wait_ge(ple_evac, G * (layer + 1))
                nc.vector.tensor_tensor(stage_tn, stage_tn, columns(ple[layer], c), ALU.mult).then_inc(chunk_evac, 1)
                dve.wait_ge(chunk_evac, c + (C_GATE[layer] + 1))
                dve.wait_ge(x1_ready, e + 1)
                if layer:
                    nc.vector.tensor_tensor(r, r, stage_tn, ALU.add).then_inc(x2_ready, 1)
                else:
                    nc.vector.tensor_tensor(stage_tn, r, stage_tn, ALU.add).then_inc(x2_sum, 1)
                    dve.wait_ge(x2_sum, e + 1)
                    nc.vector.tensor_scalar(r, stage_tn, 1.0, None, ALU.mult).then_inc(x2_ready, 1)
                    statistics(stage_tn, c)

            def x2_lo(c):
                operand_lo(c + S_X2, act1, aux_kt[0], c)

            def out_ple_gate(layer, after_out):
                n = N_OUT[layer]
                s = S_GATE[layer]
                k = 2 * G * layer
                ends = {OUT_ORDER.index((c, PC - 1)): c for c in range(G)}
                pieces(n, n, after_out | {12: [lambda: split_p(layer)]}
                       | {i: [lambda c=c, i=i: add_residual(layer, c, i + 1)] for i, c in ends.items()}, G * PC)
                pieces(N_PLE[layer], N_PLE[layer], {
                    0: [lambda: find_shift(2 * layer)]
                    + [lambda c=c: normalise(columns(res[layer], c), columns(res[layer], c)) for c in range(G)],
                    3: [lambda: full_quarter(k, 0, 0, layer, s), lambda: full_lo(s, 0),
                        lambda: full_quarter(k + 1, 1, 1, layer, s + 1), lambda: full_lo(s + 1, 1)]}, G)
                n = N_GATE[layer]
                pieces(n, n, {1: [lambda: full_quarter(k + 2, 2, 0, layer, s + 2), lambda: full_lo(s + 2, 2)],
                              3: [lambda: full_quarter(k + 3, 3, 1, layer, s + 3), lambda: full_lo(s + 3, 3)],
                              PC - 1: [lambda: add_ple(layer, 0)]})
                with dve.Fori(1, G - layer) as c:
                    pieces(c * PC + n, n, ({3: [lambda: x2_lo(c - 1)]} if layer == 0 else {})
                           | {PC - 1: [lambda: add_ple(layer, c)]})
                if layer:
                    add_ple(layer, G - 1)

            out_ple_gate(0, gate_steps(G - 1))

            def rotate(n_end, parity):
                dve.wait_ge(piece_used, n_end)
                src = acc_of(parity).rearrange("p t (h d) -> p t h d", d=DH)
                first, second = src[:, :, :, 0:HALF], src[:, :, :, HALF:DH]
                cos, sin = (cos_sin[:, i].unsqueeze(2).broadcast_to((P, TT, HG, HALF)) for i in range(2))
                nc.vector.tensor_tensor(roped_out[:, :, :, 0:HALF], first, cos, ALU.mult)
                nc.vector.tensor_tensor(roped_out[:, :, :, HALF:DH], second, cos, ALU.mult)
                nc.vector.tensor_tensor(rope_tmp[:, :, :, 0:HALF], second, sin, ALU.mult).then_inc(rope_mul, 1)
                nc.vector.tensor_tensor(rope_tmp[:, :, :, HALF:DH], first, sin, ALU.mult).then_inc(chunk_evac, 1)

            def rotate_end(k, c_evac):
                dve.wait_ge(rope_mul, k + 1)
                dve.wait_ge(chunk_evac, c_evac)
                nc.vector.tensor_tensor(roped_out[:, :, :, 0:HALF], roped_out[:, :, :, 0:HALF],
                                        rope_tmp[:, :, :, 0:HALF], ALU.subtract)
                nc.vector.tensor_tensor(roped_out[:, :, :, HALF:DH], roped_out[:, :, :, HALF:DH],
                                        rope_tmp[:, :, :, HALF:DH], ALU.add).then_inc(roped, 1)

            def q_end(c, parity):
                return {PC - 1: [lambda: rotate(c * PC + (N_Q + PC), parity),
                                 lambda: rotate_end(c, c + (C_Q + 1))]}

            def normalise_x2(c):
                normalise(columns(res[0], c), v_or_z)

            def ln_quarter(c):
                return [lambda: full_quarter(c + G, c, 1, 2, c + S_KV), lambda: full_lo(c + S_KV, c)]

            dve.wait_ge(tables_landed, 32)
            pieces(N_Q, N_Q, {2: [lambda: x2_lo(G - 1), lambda: find_shift(1), lambda: normalise_x2(0)],
                               6: ln_quarter(0)} | q_end(0, 0))
            with dve.Fori(1, G) as c:
                pieces(c * PC + N_Q, N_Q, {3: [lambda: normalise_x2(c)], 5: ln_quarter(c)} | q_end(c, c % 2))
            pieces(N_Z, N_Z, chunk_end(N_Z, 0, v_or_z[:, :, :]))
            with dve.Fori(1, G) as c:
                n = c * PC + N_Z
                pieces(n, N_Z, chunk_end(n, c % 2, v_or_z[:, :, :]))

            def k_end(n, g):
                return {PC - 1: [lambda: rotate(n + PC, 0),
                                 lambda: rotate_end(g + G, g * 2 + (C_KV + 1))]}

            def row_max(k, b):
                dve.wait_ge(scores_ready, k * 2 + (b + 1))
                for t, (lo, hi) in enumerate(((0, P), (P, SC))):
                    last = nc.vector.tensor_reduce(out=neg_max[:, b, 2 * t:2 * t + 2],
                                                   in_=aux_b[:, 2 * b:2 * b + 2, lo:hi],
                                                   axis=AX.X, op=ALU.max, negate=True)
                last.then_inc(neg_max_ready, 1)

            def divide(k, b):
                i = (k - G) * 2 + (b + 1)
                dve.wait_ge(probs_raw, i)
                nc.vector.reciprocal(row_sum[:, b], row_sum[:, b]).then_inc(inv_ready, 1)
                dve.wait_ge(inv_ready, i)
                for t, (lo, hi) in enumerate(((0, P), (P, SC))):
                    part = prob[:, b, :, lo:hi]
                    last = nc.vector.tensor_tensor(
                        part, part, row_sum[:, b, 2 * t:2 * t + 2].unsqueeze(2).broadcast_to((P, 2, hi - lo)),
                        ALU.mult)
                last.then_inc(probs_ready, 1)

            def after_v_b(k):
                return {4: [lambda: row_max(k, 0)], 5: [lambda: row_max(k, 1), lambda: divide(k, 0)],
                        6: [lambda: divide(k, 1)]}

            def after_k_b(k):
                return {4: [lambda: gate_group(k, k - G, quarter(sz_all, k - G)),
                            lambda: gated_lo(k, k - G, (k - G) + S_OUT[1])]}

            pieces(N_KV, N_KV, k_end(N_KV, 0))
            with dve.Fori(0, G - 1) as g:
                n = g * (2 * PC) + (N_KV + PC)
                pieces(n, N_KV, after_v_b(g + G) | chunk_end(n, 1, v_or_z[:, :, :]))
                pieces(n + PC, N_KV, after_k_b(g + G) | k_end(n + PC, g + 1))
            n = N_OUT[1] - PC
            pieces(n, N_KV, after_v_b(2 * G - 1) | chunk_end(n, 1, v_or_z[:, :, :]))
            out_ple_gate(1, after_k_b(2 * G - 1))

        @block.tensor
        def _(pe):
            def piece(n, r, operand, tiles, out_banks, first, final):
                pe.wait_ge(lo_ready, n + 1)
                for i, k in enumerate(tiles):
                    for t in range(TT):
                        hi, lo = (operand[:, s, k, t * P:(t + 1) * P] for s in range(2))
                        dst = out_banks[:, t]
                        begin, end = first and i == 0, final and i == PIECE_K - 1
                        nc.tensor.matmul(dst, hi, w_hi[:, r, i], start=begin, stop=False)
                        nc.tensor.matmul(dst, hi, w_lo[:, r, i], start=False, stop=False)
                        mm = nc.tensor.matmul(dst, lo, w_hi[:, r, i], start=False, stop=end)
                mm.then_inc(piece_used, 1)

            def chunk(n, base, operand, parity, c, quarters=None, after=None):
                if not isinstance(c, int) or c >= 2:
                    pe.wait_ge(chunk_evac, c - 1)
                for j in range(PC):
                    if quarters is not None and j % 2 == 0:
                        pe.wait_ge(act_ready, quarters + j // 2 + 1)
                    piece(n + j, (base + j) % SPLITS, operand, range(PIECE_K * j, PIECE_K * (j + 1)),
                          acc_of(parity), j == 0, j == PC - 1)
                    for step in (after or {}).get(j, ()):
                        step()

            def transposes(src, dst, signal):
                for i in range(HG):
                    for t in range(TT):
                        mm = nc.tensor.transpose(dst[:, i, t * P:(t + 1) * P], src[:, t, i * P:(i + 1) * P],
                                                 ident[:, :])
                mm.then_inc(signal, 1)

            def q_turn(k, c):
                pe.wait_ge(chunk_evac, c + 1)
                if not isinstance(k, int) or k > 0:
                    pe.wait_ge(gated, k)
                transposes(qn, aux_kt[0], qT_psum)

            def k_turn(k, c):
                pe.wait_ge(chunk_evac, c + 1)
                transposes(kn, aux_kt[1], kT_psum)

            def key_scores(k, b):
                pe.wait_ge(qT_ready, k + 1)
                pe.wait_ge(kT_ready, k + 1)
                for h in (2 * b, 2 * b + 1):
                    s = aux_b[:, h]
                    nc.tensor.matmul(s[:, 0:T], kT[:, h, 0:P], qT[:, h, :], start=True, stop=True,
                                     skip_group_check=True)
                    mm = nc.tensor.matmul(s[:, T:SC], kT[:, h, P:T], qT[:, h, P:T], start=False, stop=True,
                                          skip_group_check=True)
                mm.then_inc(scores_ready, 1)

            def cumulate(k, b):
                pe.wait_ge(sp_ready, k * 2 + (b + 1))
                for i, h in enumerate((2 * b, 2 * b + 1)):
                    s, sp = aux_b[:, h], prob[:, b, i]
                    for dst, lhs, rhs in ((s[:, 0:T], neg_upper, sp[:, 0:T]),
                                          (s[:, P:T], neg_ones, sp[:, T:SC]),
                                          (s[:, T:SC], neg_upper, sp[:, T:SC]),
                                          (s[:, 0:P], ident16, not_past),
                                          (s[:, T:SC], ident16, not_past)):
                        rhs = rhs[:, :]
                        mm = nc.tensor.matmul(dst, lhs[:, :], rhs, start=False, stop=True,
                                              skip_group_check=True)
                mm.then_inc(cum_ready, 1)

            def weigh_values(k, b, v, v_chunk):
                pe.wait_ge(w_ready, k * 2 + (b + 1))
                pe.wait_ge(chunk_evac, v_chunk + 1)
                for i in range(2):
                    head = slice((2 * b + i) * P, (2 * b + i + 1) * P)
                    o, w = aux_b[:, 2 * b, i * T:(i + 1) * T], prob[:, b, i]
                    nc.tensor.matmul(o, v[:, 0, head], w[:, 0:T], start=(i == 0), stop=True,
                                     skip_group_check=True)
                    mm = nc.tensor.matmul(o[:, P:T], v[:, 1, head], w[:, T:SC], start=False, stop=True,
                                          skip_group_check=True)
                mm.then_inc(pv_done, 1)

            def z_turn(k, c):
                pe.wait_ge(chunk_evac, c + 1)
                for i in range(HG):
                    for t in range(TT):
                        bank = aux_b[:, 2 * (i // 2) + 1]
                        at = (i % 2) * T + t * P
                        mm = nc.tensor.transpose(bank[:, at:at + P], zn_a[:, t, i * P:(i + 1) * P], ident[:, :])
                mm.then_inc(zT_psum, 1)

            def after_k(k, c):
                return {2: [lambda: q_turn(k, c - 1)]}

            def after_v(k, c):
                return {2: [lambda: k_turn(k, c - 1)], 4: [lambda: key_scores(k, 0)],
                        5: [lambda: key_scores(k, 1)]}

            def after_z(k, c):
                return {2: [lambda: cumulate(k, 0)], 3: [lambda: cumulate(k, 1)],
                        6: [lambda: weigh_values(k, 0, vn_a, c - 1)],
                        7: [lambda: weigh_values(k, 1, vn_a, c - 1)]}

            def z_step(k, c):
                return {2: [lambda: z_turn(k, c)]}

            pe.wait_ge(consts_done, 13)
            chunk(0, 0, act0, 0, 0, quarters=S_X)
            chunk(PC, 0, act0, 1, 1, after=after_k(0, 1))
            with pe.Fori(0, G - 1) as g:
                n = g * (4 * PC) + 2 * PC
                c = g * 4 + 2
                chunk(n, 0, act0, 0, c, after=after_v(g, c))
                chunk(n + PC, 0, act0, 1, c + 1, after=after_z(g, c + 1))
                chunk(n + 2 * PC, 0, act0, 0, c + 2, after=z_step(g, c + 1))
                chunk(n + 3 * PC, 0, act0, 1, c + 3, after=after_k(g + 1, c + 3))
            c = C_OUT[0] - 2
            chunk(c * PC, 0, act0, 0, c, after=after_v(G - 1, c))
            chunk((c + 1) * PC, 0, act0, 1, c + 1, after=after_z(G - 1, c + 1))

            def ln_turn(k, c, pair, layer, src):
                pe.wait_ge(normed, k + 1)
                transposes(src if c is None else columns(src, c), aux_kt[pair], lnT_psum)

            def out_projection(layer, after_out):
                for i, (c, j) in enumerate(OUT_ORDER):
                    n = N_OUT[layer] + i
                    if j == 0:
                        pe.wait_ge(chunk_evac, C_OUT[layer] + c - 1)
                    if c == 0 and j % 2 == 0:
                        pe.wait_ge(act_ready, S_OUT[layer] + j // 2 + 1)
                    piece(n, n % SPLITS, act1, range(PIECE_K * j, PIECE_K * (j + 1)), acc_of(c % 2),
                          j == 0, j == PC - 1)
                    for step in after_out.get(i, ()):
                        step()

            def ple_and_gate(layer):
                k = 2 * G * layer
                s = S_GATE[layer]
                pe.wait_ge(p_ready, layer + 1)
                for c in range(G):
                    n = N_PLE[layer] + c
                    if c >= 2:
                        pe.wait_ge(chunk_evac, C_OUT[layer] + c + 1)
                    banks = acc_of(c % 2) if c >= 2 else \
                        aux[:, c * 2 * COLS:(c + 1) * 2 * COLS].rearrange(tokens, t=TT)
                    piece(n, n % SPLITS, act0, range(KT - PIECE_K, KT), banks, True, True)
                pe.wait_ge(ple_evac, layer * G + 2)
                ln_turn(k, 0, 0, layer, res[layer])
                ln_turn(k + 1, 1, 1, layer, res[layer])
                n, c0 = N_GATE[layer], C_GATE[layer]

                def later_turn(i):
                    pe.wait_ge(full_ready, k + i - 1)
                    ln_turn(k + i, i, i % 2, layer, res[layer])

                pe.wait_ge(ple_evac, (layer + 1) * G)
                chunk(n, n, act0, 0, c0, quarters=s,
                      after={1: [lambda: later_turn(2)], 3: [lambda: later_turn(3)]})
                with pe.Fori(1, G) as c:
                    chunk(c * PC + n, n, act0, c % 2, c + c0,
                          after={3: [lambda: x2_turn(c - 1)]} if layer == 0 else None)

            def x2_turn(c):
                pe.wait_ge(x2_ready, c + 1)
                pe.wait_ge(act_ready, c + S_X2)
                transposes(stage_tn, aux_kt[0], x2T_psum)

            out_projection(0, z_step(G - 1, C_OUT[0] - 1))
            ple_and_gate(0)

            def ln_step(c):
                if not isinstance(c, int):
                    pe.wait_ge(full_ready, c + G)
                ln_turn(c + G, None, 1, 0, v_or_z)

            def q_turn_b(c):
                pe.wait_ge(roped, c + 1)
                if isinstance(c, int) and c == 0:
                    pe.wait_ge(act_ready, S_X2 + G)
                else:
                    pe.wait_ge(qT_ready, c + G)
                transposes(roped_rows, aux_kt[0], qT_psum)

            def z_turn_b(c):
                pe.wait_ge(chunk_evac, c + (C_Z + 1))
                pe.wait_ge(sz_ready, c + G)
                transposes(v_or_z, aux_kt[0], zT_psum)

            def k_turn_b(k):
                pe.wait_ge(roped, k + 1)
                pe.wait_ge(gated, k)
                transposes(roped_rows, aux_kt[1], kT_psum)

            def query_scores(k, b):
                pe.wait_ge(kT_ready, k + 1)
                pe.wait_ge(q_group_ready, (k - G) + 1)
                for h in (2 * b, 2 * b + 1):
                    s, first = aux_b[:, h], True
                    for dst, lhs, rhs in ((s[:, 0:P], qT[:, h, 0:P], kT[:, h, 0:P]),
                                          (s[:, P:SC], qT[:, h, P:T], kT[:, h, :]),
                                          (s[:, 0:P], ident16[:, :], future[:, :]),
                                          (s[:, T:SC], ident16[:, :], future[:, :])):
                        mm = nc.tensor.matmul(dst, lhs, rhs, start=first, stop=True, skip_group_check=True)
                        first = False
                mm.then_inc(scores_ready, 1)

            def probs_turn(k, b):
                pe.wait_ge(probs_ready, (k - G) * 2 + (b + 1))
                for i in range(2):
                    for s in range(3):
                        mm = nc.tensor.transpose(aux_b[:, 2 * b + i, s * P:(s + 1) * P],
                                                 prob[:, b, i, s * P:(s + 1) * P], ident[:, :])
                mm.then_inc(probsT_psum, 1)

            chunk(N_Q, N_Q, act1, 0, C_Q, quarters=S_X2,
                  after={2: [lambda: x2_turn(G - 1)], 6: [lambda: ln_step(0)]})
            with pe.Fori(1, G) as c:
                chunk(c * PC + N_Q, N_Q, act1, c % 2, c + C_Q,
                      after={2: [lambda: q_turn_b(c - 1)], 5: [lambda: ln_step(c)]})
            chunk(N_Z, N_Z, act1, 0, C_Z, after={2: [lambda: q_turn_b(G - 1)]})
            with pe.Fori(1, G) as c:
                chunk(c * PC + N_Z, N_Z, act1, c % 2, c + C_Z, after={2: [lambda: z_turn_b(c - 1)]})

            def after_v_b(k):
                return {2: [lambda: k_turn_b(k)], 4: [lambda: query_scores(k, 0)],
                        5: [lambda: query_scores(k, 1)]}

            def after_k_b(k, v_chunk):
                v = v_or_z
                return {0: [lambda: probs_turn(k, 0)], 1: [lambda: probs_turn(k, 1)],
                        3: [lambda: weigh_values(k, 0, v, v_chunk)],
                        4: [lambda: weigh_values(k, 1, v, v_chunk)]}

            chunk(N_KV, N_KV, act0, 0, C_KV, quarters=S_KV, after={2: [lambda: z_turn_b(G - 1)]})
            pe.wait_ge(sz_ready, 2 * G)
            with pe.Fori(0, G - 1) as g:
                n = g * (2 * PC) + (N_KV + PC)
                c = g * 2 + (C_KV + 1)
                chunk(n, N_KV, act0, 1, c, after=after_v_b(g + G))
                chunk(n + PC, N_KV, act0, 0, c + 1, after=after_k_b(g + G, c))
            c = C_OUT[1] - 1
            chunk(N_OUT[1] - PC, N_KV, act0, 1, c, after=after_v_b(2 * G - 1))
            out_projection(1, after_k_b(2 * G - 1, c))
            ple_and_gate(1)


def kernel(x, p, w_in_a, w_out_a, w_kv, ln_kv_g, ln_kv_b, w_in_b, w_out_b, ln_g, ln_b, w_ple, w_ple_gate):
    import concourse.bacc as bacc
    from concourse.bass_utils import run_bass_kernel_spmd

    x, p, ln_g, ln_b, ln_kv_g, ln_kv_b = (np.asarray(a) for a in (x, p, ln_g, ln_b, ln_kv_g, ln_kv_b))
    depth, _, seq, d = p.shape[0], p.shape[1], x.shape[1], x.shape[2]
    tiles = d // P
    half = P // 2
    inv_freq = np.float32(10000.0) ** (-np.arange(half, dtype=np.float32) / np.float32(half))
    angle = np.arange(seq, dtype=np.float32)[:, None] * inv_freq[None, :]
    rope = np.stack([np.cos(angle), np.sin(angle)]).astype(np.float32)
    by_feature = np.stack([np.stack([ln_g[0], ln_b[0]]), np.stack([ln_g[1], ln_b[1]]),
                           np.stack([ln_kv_g, ln_kv_b])])
    arrays = {
        "xt": np.ascontiguousarray(x[0].T),
        "x": np.ascontiguousarray(x[0]),
        "pt": np.ascontiguousarray(p[:, 0].transpose(0, 2, 1)),
        "w_in_a": np.asarray(w_in_a), "w_out_a": np.asarray(w_out_a), "w_kv": np.asarray(w_kv),
        "w_in_b": np.asarray(w_in_b), "w_out_b": np.asarray(w_out_b), "w_ple": np.asarray(w_ple),
        "w_ple_gate": np.asarray(w_ple_gate),
        "ln_rows": np.ascontiguousarray(np.stack([ln_g, ln_b], axis=1)),
        "ln_cols": np.ascontiguousarray(by_feature.reshape(3, 2, tiles, P).transpose(3, 0, 1, 2)),
        "rope": np.ascontiguousarray(rope.reshape(2, seq // P, P, half).transpose(2, 0, 1, 3)),
    }
    assert depth == 2
    nc = bacc.Bacc("TRN2", target_bir_lowering=False, num_devices=1)
    args = [nc.dram_tensor(f"in_{n}", a.shape, mybir.dt.from_np(a.dtype), kind="ExternalInput").ap()
            for n, a in arrays.items()]
    out = nc.dram_tensor("out", (seq, d), F32, kind="ExternalOutput").ap()
    build(nc, *args, out)
    r = run_bass_kernel_spmd(nc, [{f"in_{n}": a for n, a in arrays.items()}], core_ids=[0])
    return np.asarray(r.results[0]["out"]).reshape(1, seq, d)
```

```python
import math
from contextlib import ExitStack

import concourse.bass as bass
import numpy as np
from concourse import mybir

F32 = mybir.dt.float32
F32R = mybir.dt.float32r
BF16 = mybir.dt.bfloat16
ALU = mybir.AluOpType
ACT = mybir.ActivationFunctionType
AX = mybir.AxisListType

P = 128
NEG = -1e30
LN_EPS = 1e-5
COLS = 512
PIECE_K = 2
RAWS = 4
SPLITS = 8
WARM_UPS = 14


def build(nc, xt, x, pt, w_in_a, w_out_a, w_kv, w_in_b, w_out_b, w_ple, w_ple_gate,
          ln_rows, ln_cols, rope, out):
    D, T = xt.shape
    TT = T // P
    KT = D // P
    DH = P
    HG = COLS // DH
    G = D // COLS
    PC = KT // PIECE_K
    HALF = DH // 2
    LAYERS = w_ple.shape[0]
    ALPHA = (2.0 * LAYERS) ** 0.25
    SCALE = 1.0 / math.sqrt(DH)
    SC = 3 * P
    assert TT == 2 and PC == SPLITS and LAYERS == 2 and HG == 4 and G == 4

    N_QKVZ = 0
    N_OUT = [N_QKVZ + 4 * G * PC, 0]
    N_PLE = [N_OUT[0] + G * PC, 0]
    N_GATE = [N_PLE[0] + G, 0]
    N_Q = N_GATE[0] + G * PC
    N_Z = N_Q + G * PC
    N_KV = N_Z + G * PC
    N_OUT[1] = N_KV + 2 * G * PC
    N_PLE[1] = N_OUT[1] + G * PC
    N_GATE[1] = N_PLE[1] + G
    PIECES = N_GATE[1] + G * PC
    C_QKVZ = 0
    C_OUT = [C_QKVZ + 4 * G, 0]
    C_GATE = [C_OUT[0] + G, 0]
    C_Q = C_GATE[0] + G
    C_Z = C_Q + G
    C_KV = C_Z + G
    C_OUT[1] = C_KV + 2 * G
    C_GATE[1] = C_OUT[1] + G
    S_X = 0
    S_OUT = [PC, PC + 4 * G]
    S_GATE = [PC + G, PC + 5 * G]
    S_X2 = PC + 2 * G
    S_KV = PC + 3 * G
    FIRST_ROWS = PC - PIECE_K
    OUT_ORDER = ([(c, j) for c in (0, 1) for j in range(FIRST_ROWS)]
                 + [(c, j) for c in (0, 1) for j in range(FIRST_ROWS, PC)]
                 + [(c, j) for c in range(2, G) for j in range(PC)])

    with ExitStack() as ctx:
        def sb(name, shape, dt=F32):
            return ctx.enter_context(nc.sbuf_tensor(name, [P, *shape], dt))

        def sem(name):
            return ctx.enter_context(nc.semaphore(name))

        raw = sb("raw", [RAWS, PIECE_K, COLS])
        w_hi = sb("w_hi", [SPLITS, PIECE_K, COLS], F32R)
        w_lo = sb("w_lo", [SPLITS, PIECE_K, COLS], F32R)
        act0 = sb("act0", [2, KT, T], F32R)
        act1 = sb("act1", [2, KT, T], F32R)
        big0 = sb("big0", [TT * D])
        big1_at = nc.sbuf_base
        big1 = sb("big1", [TT * D])
        sp_parts = nc.alloc_sbuf_tensor_at("sp_parts", [P, 2, 2, 2, SC], F32R, offset=big1_at)
        heads = sb("heads", [3 * HG * T + 2 * 2 * SC])
        v_or_z = sb("v_or_z", [TT, COLS])
        stage = sb("stage", [HG * T])
        ident = sb("ident", [P])
        neg_upper = sb("neg_upper", [P], F32R)
        neg_ones = sb("neg_ones", [P], F32R)
        past = sb("past", [P])
        ident16 = sb("ident16", [P], BF16)
        not_past = sb("not_past", [P], BF16)
        future = sb("future", [P], BF16)
        cos_sin = sb("cos_sin", [2, TT, HALF])
        ln_col = sb("ln_col", [3, 2, KT])
        stats = sb("stats", [TT, G, 6])
        moments = sb("moments", [TT, 2])
        var_eps = sb("var_eps", [TT])
        minus_half = sb("minus_half", [TT])
        rstd = sb("rstd", [TT])
        shift = sb("shift", [TT])
        neg_max = sb("neg_max", [2, 2 * TT])
        row_sum = sb("row_sum", [2, 2 * TT])
        acc = ctx.enter_context(nc.psum_tensor("acc", [P, 4 * COLS], F32))
        aux = ctx.enter_context(nc.psum_tensor("aux", [P, 4 * COLS], F32))
        x2_spill = nc.dram_tensor("x2_spill", [T, D], F32).ap()

        tokens = "p (t n) -> p t n"
        qn, kn, vn_a, zn_a = (big0[:, i * TT * COLS:(i + 1) * TT * COLS].rearrange(tokens, t=TT)
                              for i in range(4))
        q_all = big0[:, :].rearrange("p (h t) -> p h t", t=T)
        sz_all = big1[:, :].rearrange("p (h t) -> p h t", t=T)
        x_raw = big1[:, :].rearrange("p (k t) -> p k t", t=T)
        res = [big1[:, :].rearrange(tokens, t=TT), big0[:, :].rearrange(tokens, t=TT)]
        ple = [big0[:, :].rearrange(tokens, t=TT), big1[:, :].rearrange(tokens, t=TT)]
        HT = HG * T
        kT = heads[:, 0:HT].rearrange("p (h t) -> p h t", t=T)
        qT = heads[:, HT:2 * HT].rearrange("p (h t) -> p h t", t=T)
        prob = heads[:, 2 * HT:2 * HT + 4 * SC].rearrange("p (b h c) -> p b h c", b=2, c=SC)
        gt = heads[:, 2 * HT + 4 * SC:].rearrange("p (h t) -> p h t", t=T)
        gain = heads[:, 0:D]
        offset = heads[:, D:2 * D]
        rope_tmp = heads[:, 0:HT].rearrange("p (t h d) -> p t h d", t=TT, d=DH)
        roped_out = heads[:, 2 * HT:3 * HT].rearrange("p (t h d) -> p t h d", t=TT, d=DH)
        roped_rows = heads[:, 2 * HT:3 * HT].rearrange(tokens, t=TT)
        stage_kt = stage[:, :].rearrange("p (k t) -> p k t", t=T)
        stage_tn = stage[:, :].rearrange(tokens, t=TT)
        p_raw = stage[:, 0:PIECE_K * T].rearrange("p (k t) -> p k t", t=T)
        neg_upper_raw, neg_ones_raw = stage[:, 0:P], stage[:, P:2 * P]
        p_act = act0[:, :, KT - PIECE_K:KT, :]
        aux_b = aux[:, :].rearrange("p (b n) -> p b n", n=COLS)
        aux_kt = [aux[:, 0:HT].rearrange("p (k t) -> p k t", t=T),
                  aux[:, HT:2 * HT].rearrange("p (k t) -> p k t", t=T)]

        def acc_of(parity):
            if isinstance(parity, int):
                return acc[:, parity * 2 * COLS:(parity + 1) * 2 * COLS].rearrange(tokens, t=TT)
            return acc[:, bass.ts(parity, 2 * COLS)].rearrange(tokens, t=TT)

        def quarter(ap, c):
            return ap[:, HG * c:HG * c + HG] if isinstance(c, int) else ap[:, bass.ds(c * HG, HG)]

        def columns(ap, c):
            return ap[:, :, COLS * c:COLS * c + COLS] if isinstance(c, int) else ap[:, :, bass.ts(c, COLS)]

        def scores_of(b):
            return aux_b[:, 2 * b:2 * b + 2, 0:SC]

        w_landed = [sem(f"dma_w_landed{i}") for i in range(RAWS)]
        x_landed = [sem(f"dma_x_landed{i}") for i in range(PC)]
        tables_landed = sem("dma_tables_landed")
        res_landed = [sem(f"dma_res_landed{i}") for i in range(G)]
        p_landed = sem("dma_p_landed")
        ln_rows_landed = sem("dma_ln_rows_landed")
        x2_spilled = sem("dma_x2_spilled")
        out_stored = sem("dma_out_stored")
        consts_done = sem("pool_consts_done")
        rstd_done = sem("pool_rstd_done")
        gained = sem("pool_gained")
        x1_ready = sem("pool_x1_ready")
        q_group_ready = sem("pool_q_group_ready")
        masks_done = sem("act_masks_done")
        hi_ready = sem("act_hi_ready")
        act_hi = sem("act_operand_hi")
        p_hi = sem("act_p_hi")
        qT_ready = sem("act_qT_ready")
        kT_ready = sem("act_kT_ready")
        abs_done = sem("act_abs_done")
        exp_done = sem("act_exp_done")
        ln_done = sem("act_ln_done")
        probs_raw = sem("act_probs_raw")
        w_ready = sem("act_w_ready")
        sp_hi = sem("act_sp_hi")
        sz_ready = sem("act_sz_ready")
        ple_evac = sem("act_ple_evac")
        sig_ready = sem("act_sig_ready")
        normed_1 = sem("act_normed_1")
        lo_ready = sem("dve_lo_ready")
        act_ready = sem("dve_operand_ready")
        p_ready = sem("dve_p_ready")
        chunk_evac = sem("dve_chunk_evac")
        tile_0_added = sem("dve_tile_0_added")
        sp_raw = sem("dve_sp_raw")
        sp_ready = sem("dve_sp_ready")
        sp_lo = sem("dve_sp_lo")
        gated = sem("dve_gated")
        rope_mul = sem("dve_rope_mul")
        roped = sem("dve_roped")
        neg_max_ready = sem("dve_neg_max_ready")
        inv_ready = sem("dve_inv_ready")
        probs_ready = sem("dve_probs_ready")
        stats_done = sem("dve_stats_done")
        moments_done = sem("dve_moments_done")
        var_done = sem("dve_var_done")
        shift_done = sem("dve_shift_done")
        normed_0 = sem("dve_normed_0")
        full_ready = sem("dve_full_ready")
        x2_sum = sem("dve_x2_sum")
        x2_ready = sem("dve_x2_ready")
        piece_used = sem("pe_piece_used")
        tile_0_done = sem("pe_tile_0_done")
        qT_psum = sem("pe_qT_psum")
        kT_psum = sem("pe_kT_psum")
        scores_ready = sem("pe_scores_ready")
        cum_ready = sem("pe_cum_ready")
        probsT_psum = sem("pe_probsT_psum")
        pv_done = sem("pe_pv_done")
        zT_psum = sem("pe_zT_psum")
        lnT_psum = sem("pe_lnT_psum")
        x2T_psum = sem("pe_x2T_psum")

        block = ctx.enter_context(nc.Block())

        @block.sync
        def _(sp):
            def load(n, r, matrix, j, c):
                rows = matrix[j * PIECE_K * P:(j + 1) * PIECE_K * P, :]
                cols = rows[:, c * COLS:(c + 1) * COLS] if isinstance(c, int) else rows[:, bass.ts(c, COLS)]
                if not isinstance(n, int) or n >= RAWS:
                    sp.wait_ge(lo_ready, n - RAWS + 1)
                sp.dma_start(raw[:, r % RAWS], cols.rearrange("(k p) n -> p k n", p=P)) \
                    .then_inc(w_landed[r % RAWS], 16)

            def load_chunk(n, base, matrix, c):
                for j in range(PC):
                    load(n + j, (base + j) % SPLITS, matrix, j, c)

            wa = w_in_a[0]
            for j in range(PC):
                sp.dma_start(x_raw[:, PIECE_K * j:PIECE_K * (j + 1), :],
                             xt[j * PIECE_K * P:(j + 1) * PIECE_K * P, :].rearrange("(k p) t -> p k t", p=P)) \
                    .then_inc(x_landed[j], 16)
                load(j, j, wa, j, 0)
            load_chunk(PC, 0, wa, G)
            with sp.Fori(0, G - 1) as g:
                n = g * (4 * PC) + 2 * PC
                load_chunk(n, 0, wa, g + 2 * G)
                load_chunk(n + PC, 0, wa, g + 3 * G)
                load_chunk(n + 2 * PC, 0, wa, g + 1)
                load_chunk(n + 3 * PC, 0, wa, g + 1 + G)
            load_chunk(N_OUT[0] - 2 * PC, 0, wa, 3 * G - 1)
            load_chunk(N_OUT[0] - PC, 0, wa, 4 * G - 1)

            def load_out_ple_gate(layer, w_out):
                n = N_OUT[layer]
                for i, (c, j) in enumerate(OUT_ORDER):
                    load(n + i, (n + i) % SPLITS, w_out, j, c)
                for c in range(G):
                    load(N_PLE[layer] + c, (N_PLE[layer] + c) % SPLITS, w_ple[layer], 0, c)
                with sp.Fori(0, G) as c:
                    load_chunk(c * PC + N_GATE[layer], N_GATE[layer], w_ple_gate[layer], c)

            load_out_ple_gate(0, w_out_a[0])
            with sp.Fori(0, 2 * G) as c:
                load_chunk(c * PC + N_Q, N_Q, w_in_b[0], c)
            with sp.Fori(0, G) as g:
                n = g * (2 * PC) + N_KV
                load_chunk(n, N_KV, w_kv, g)
                load_chunk(n + PC, N_KV, w_kv, g + G)
            load_out_ple_gate(1, w_out_b[0])
            with sp.Fori(0, G - 1) as c:
                sp.wait_ge(x2_ready, c + (G + 1))
                sp.dma_start(out[:, bass.ts(c, COLS)].rearrange("(t p) n -> p t n", p=P),
                             columns(res[1], c)).then_inc(out_stored, 16)
            for t in range(TT):
                sp.wait_ge(x2_ready, 2 * G + t)
                sp.dma_start(out[t * P:(t + 1) * P, (G - 1) * COLS:], columns(res[1], G - 1)[:, t]) \
                    .then_inc(out_stored, 16)
            sp.wait_ge(out_stored, 16 * (G - 1 + TT))

        @block.gpsimd
        def _(pool):
            for ap, value in ((ident[:, :], 0.0), (neg_upper_raw, -1.0), (neg_ones_raw, -1.0), (past[:, :], 1.0),
                              (not_past[:, :], 0.0), (future[:, :], 0.0), (minus_half[:, :], -0.5)):
                nc.gpsimd.memset(ap, value).then_inc(consts_done, 1)
            pool.wait_ge(consts_done, 7)
            for ap, op, fill, step, mult in ((ident[:, :], ALU.not_equal, 1.0, -1, 1),
                                             (neg_upper_raw, ALU.is_ge, 0.0, -1, 1),
                                             (past[:, :], ALU.is_gt, 0.0, 1, -1),
                                             (not_past[:, :], ALU.is_gt, NEG, 1, -1),
                                             (future[:, :], ALU.is_ge, NEG, -1, 1)):
                nc.gpsimd.affine_select(out=ap, in_=ap, compare_op=op, fill=fill, base=0,
                                        pattern=[[step, P]], channel_multiplier=mult) \
                    .then_inc(consts_done, 1)
            pool.wait_ge(consts_done, 8)
            nc.gpsimd.tensor_copy(ident16[:, :], ident[:, :]).then_inc(consts_done, 1)

            def load_res(layer, src):
                for c in range(G):
                    pool.dma_start(columns(res[layer], c),
                                   src[:, c * COLS:(c + 1) * COLS].rearrange("(t p) n -> p t n", p=P)) \
                        .then_inc(res_landed[c], 16)

            def load_p(layer):
                pool.dma_start(p_raw, pt[layer].rearrange("(k p) t -> p k t", p=P)).then_inc(p_landed, 16)

            def load_ln_rows(layer):
                for i, row in enumerate((gain, offset)):
                    pool.dma_start(row, ln_rows[layer, i:i + 1, :].broadcast_to((P, D))) \
                        .then_inc(ln_rows_landed, 16)

            def inverse_std(k):
                pool.wait_ge(var_done, k + 1)
                nc.gpsimd.tensor_tensor(rstd[:, :], var_eps[:, :], minus_half[:, :], ALU.pow) \
                    .then_inc(rstd_done, 1)

            def gain_and_offset(layer):
                pool.wait_ge(ln_rows_landed, 32 * (layer + 1))
                for c in range(G):
                    x1 = columns(res[layer], c)
                    row = lambda r: r[:, c * COLS:(c + 1) * COLS].unsqueeze(1).broadcast_to((P, TT, COLS))
                    pool.wait_ge(lnT_psum, (2 * G if layer else 0) + c + 1)
                    nc.gpsimd.tensor_tensor(x1, x1, row(gain), ALU.mult).then_inc(gained, 1)
                    pool.wait_ge(gained, layer * G + c + 1)
                    nc.gpsimd.tensor_tensor(x1, x1, row(offset), ALU.add).then_inc(x1_ready, 1)

            pool.wait_ge(act_ready, PC)
            pool.wait_ge(masks_done, 1)
            pool.wait_ge(piece_used, 1)
            load_p(0)
            pool.dma_start(cos_sin[:, :, :, :], rope).then_inc(tables_landed, 16)
            pool.dma_start(ln_col[:, :, :, :], ln_cols).then_inc(tables_landed, 16)
            pool.wait_ge(cum_ready, 2 * G)
            load_res(0, x)
            pool.wait_ge(act_ready, S_OUT[0] + G)
            load_ln_rows(0)
            inverse_std(0)
            gain_and_offset(0)
            with pool.Fori(0, G) as c:
                pool.wait_ge(x2_ready, c + 1)
                pool.dma_start(x2_spill[:, bass.ts(c, COLS)].rearrange("(t p) n -> p t n", p=P),
                               columns(res[0], c)).then_inc(x2_spilled, 16)
            inverse_std(1)
            with pool.Fori(0, G) as g:
                pool.wait_ge(qT_ready, g + (G + 1))
                pool.wait_ge(scores_ready, g * 2 + 2 * G)
                nc.gpsimd.tensor_copy(qT[:, :, :], quarter(q_all, g)).then_inc(q_group_ready, 1)
            pool.wait_ge(q_group_ready, G)
            pool.wait_ge(x2_spilled, 16 * G)
            load_res(1, x2_spill)
            pool.wait_ge(act_ready, S_KV + G)
            load_p(1)
            pool.wait_ge(act_ready, S_OUT[1] + G)
            load_ln_rows(1)
            inverse_std(2)
            gain_and_offset(1)

        @block.scalar
        def _(act):
            def split(n, r):
                act.wait_ge(w_landed[r % RAWS], n * 4 + (16 - 4 * (r % RAWS)))
                if not isinstance(n, int) or n >= SPLITS:
                    act.wait_ge(piece_used, n - SPLITS + 1)
                nc.scalar.activation(w_hi[:, r], raw[:, r % RAWS], ACT.Copy).then_inc(hi_ready, 1)

            def pieces(n, base, after=None, count=PC, before=None):
                for j in range(count):
                    for step in (before or {}).get(j, ()):
                        step()
                    if not isinstance(n, int) or n + j + SPLITS < PIECES:
                        split(n + (j + SPLITS), (base + j) % SPLITS)
                    for step in (after or {}).get(j, ()):
                        step()

            def operand_hi(dst, src, c):
                nc.scalar.activation(quarter(dst[:, 0], c), src, ACT.Copy).then_inc(act_hi, 1)

            def copy_qT(k, dst):
                act.wait_ge(qT_psum, k + 1)
                nc.scalar.activation(dst, aux_kt[0], ACT.Copy, scale=SCALE).then_inc(qT_ready, 1)

            def copy_kT(k):
                act.wait_ge(kT_psum, k + 1)
                nc.scalar.activation(kT, aux_kt[1], ACT.Copy).then_inc(kT_ready, 1)

            def exp_abs(k, b):
                act.wait_ge(scores_ready, k * 2 + (b + 1))
                nc.scalar.activation(prob[:, b], scores_of(b), ACT.Abs).then_inc(abs_done, 1)
                act.wait_ge(abs_done, k * 2 + (b + 1))
                nc.scalar.activation(prob[:, b], prob[:, b], ACT.Exp, scale=-1.0).then_inc(exp_done, 1)

            def log_1p(k):
                for b in range(2):
                    act.wait_ge(exp_done, k * 2 + (b + 1))
                    nc.scalar.activation(prob[:, b], prob[:, b], ACT.Ln, bias=1.0).then_inc(ln_done, 1)

            def softplus_hi(k, b):
                act.wait_ge(sp_ready, k * 2 + (b + 1))
                nc.scalar.activation(sp_parts[:, 0, b], prob[:, b], ACT.Copy).then_inc(sp_hi, 1)

            def stick_weights(k, b):
                act.wait_ge(cum_ready, k * 2 + (b + 1))
                nc.scalar.activation(prob[:, b], scores_of(b), ACT.Exp).then_inc(w_ready, 1)

            def silu_z(k, dst, src):
                act.wait_ge(zT_psum, k + 1)
                nc.scalar.activation(dst, src, ACT.Silu).then_inc(sz_ready, 1)

            def gated_hi(k, c):
                act.wait_ge(gated, k + 1)
                operand_hi(act1, gt, c)

            def silu_z_group(k):
                act.wait_ge(act_ready, k + S_OUT[0])
                silu_z(k, gt, aux[:, :].rearrange("p (b s n) -> p b s n", b=2, s=2)[:, :, 1])

            def softmax_exp(k, b):
                act.wait_ge(neg_max_ready, (k - G) * 2 + (b + 1))
                for t in range(TT):
                    for h in range(2):
                        lo, hi = (0, P) if t == 0 else (P, SC)
                        i = 2 * t + h
                        last = nc.scalar.activation(prob[:, b, h, lo:hi], aux_b[:, 2 * b + h, lo:hi], ACT.Exp,
                                                    bias=neg_max[:, b, i:i + 1],
                                                    accum_out=row_sum[:, b, i:i + 1])
                last.then_inc(probs_raw, 1)

            def copy_probsT(k, b):
                act.wait_ge(probsT_psum, (k - G) * 2 + (b + 1))
                nc.scalar.activation(prob[:, b], scores_of(b), ACT.Copy).then_inc(w_ready, 1)

            for j in range(PC):
                act.wait_ge(x_landed[j], 16)
                part = slice(PIECE_K * j, PIECE_K * (j + 1))
                nc.scalar.activation(act0[:, 0, part], x_raw[:, part], ACT.Copy).then_inc(act_hi, 1)
                split(j, j)

            act.wait_ge(consts_done, 13)
            nc.scalar.activation(neg_upper[:, :], neg_upper_raw, ACT.Copy)
            nc.scalar.activation(neg_ones[:, :], neg_ones_raw, ACT.Copy).then_inc(masks_done, 1)

            def after_k(k):
                return {4: [lambda: copy_qT(k, qT)]}

            def after_v(k):
                return {2: [lambda: copy_kT(k)], 4: [lambda: exp_abs(k, 0)],
                        5: [lambda: exp_abs(k, 1), lambda: log_1p(k)],
                        6: [lambda: softplus_hi(k, 0)], 7: [lambda: softplus_hi(k, 1)]}

            def after_z(k):
                return {2: [lambda: stick_weights(k, 0)], 3: [lambda: stick_weights(k, 1)]}

            def gate_group(k):
                return {2: [lambda: silu_z_group(k)], 3: [lambda: gated_hi(k, k)]}

            pieces(0, 0)
            pieces(PC, 0, after_k(0))
            with act.Fori(0, G - 1) as g:
                n = g * (4 * PC) + 2 * PC
                pieces(n, 0, after_v(g))
                pieces(n + PC, 0, after_z(g))
                pieces(n + 2 * PC, 0, gate_group(g))
                pieces(n + 3 * PC, 0, after_k(g + 1))
            pieces(N_OUT[0] - 2 * PC, 0, after_v(G - 1))
            pieces(N_OUT[0] - PC, 0, after_z(G - 1))

            def split_p(layer):
                act.wait_ge(p_landed, 16 * (layer + 1))
                act.wait_ge(piece_used, N_OUT[layer])
                nc.scalar.activation(p_act[:, 0], p_raw, ACT.Copy).then_inc(p_hi, 1)

            def ple_out(layer, c):
                act.wait_ge(piece_used, N_PLE[layer] + c + 1)
                src = (aux if c < 2 else acc)[:, (c % 2) * 2 * COLS:(c % 2 + 1) * 2 * COLS]
                nc.scalar.activation(columns(ple[layer], c), src.rearrange(tokens, t=TT), ACT.Copy) \
                    .then_inc(ple_evac, 1)

            def normalise(k, src, dst):
                act.wait_ge(shift_done, k + 1)
                nc.scalar.activation(dst[:, 1], src[:, 1], ACT.Identity, bias=shift[:, 1:2],
                                     scale=rstd[:, 1:2]).then_inc(normed_1, 1)

            def full_hi(k, c):
                act.wait_ge(full_ready, k + 1)
                operand_hi(act0, stage_kt, c)

            def sigmoid_gate(layer, c, parity):
                act.wait_ge(piece_used, c * PC + (N_GATE[layer] + PC))
                if not isinstance(c, int) or c + layer > 0:
                    act.wait_ge(x2_ready, c + layer * G)
                if layer == 0 and not isinstance(c, int):
                    act.wait_ge(x2T_psum, c)
                nc.scalar.activation(stage_tn, acc_of(parity), ACT.Sigmoid).then_inc(sig_ready, 1)

            def x2_hi(c):
                act.wait_ge(x2T_psum, c + 1)
                operand_hi(act1, aux_kt[0], c)

            def out_ple_gate(layer, after_out):
                n = N_OUT[layer]
                pieces(n, n, after_out | {12: [lambda: split_p(layer)]}, G * PC)
                n = N_PLE[layer]
                k = 2 * G * layer
                x1 = [columns(res[layer], c) for c in range(G)]
                ple_step, full_step = ([lambda c=c: ple_out(layer, c) for c in range(G)],
                                       [lambda c=c: full_hi(k + c, c) for c in range(G)])
                pieces(n, n, count=G, before={
                    0: ple_step[0:1] + [lambda r=r: normalise(2 * layer, r, r) for r in x1]
                    + ple_step[1:2] + full_step[0:1] + ple_step[2:3] + full_step[1:2] + ple_step[3:4],
                    2: full_step[2:3]})
                n = N_GATE[layer]
                pieces(n, n, {PC - 1: [lambda: sigmoid_gate(layer, 0, 0)]}, before={0: full_step[3:4]})
                with act.Fori(1, G - layer) as c:
                    pieces(c * PC + n, n, ({3: [lambda: x2_hi(c - 1)]} if layer == 0 else {})
                           | {PC - 1: [lambda: sigmoid_gate(layer, c, c % 2)]})
                if layer:
                    for t in range(TT):
                        act.wait_ge(*((tile_0_done, LAYERS + 1) if t == 0 else (piece_used, PIECES)))
                        act.wait_ge(x2_ready, 2 * G - 1)
                        nc.scalar.activation(stage_tn[:, t], acc_of((G - 1) % 2)[:, t], ACT.Sigmoid) \
                            .then_inc(sig_ready, 1)

            out_ple_gate(0, gate_group(G - 1))

            def ln_hi(c):
                full_hi(c + G, c)

            def normalise_x2(c):
                normalise(1, columns(res[0], c), v_or_z)

            pieces(N_Q, N_Q, {2: [lambda: x2_hi(G - 1)], 3: [lambda: normalise_x2(0)], 6: [lambda: ln_hi(0)]})
            with act.Fori(1, G) as c:
                pieces(c * PC + N_Q, N_Q, {2: [lambda: copy_qT(c + (G - 1), quarter(q_all, c - 1))],
                                           3: [lambda: normalise_x2(c)], 5: [lambda: ln_hi(c)]})
            pieces(N_Z, N_Z, {2: [lambda: copy_qT(2 * G - 1, quarter(q_all, G - 1))]})
            act.wait_ge(x2_spilled, 16 * G)
            with act.Fori(1, G) as c:
                pieces(c * PC + N_Z, N_Z,
                       {2: [lambda: silu_z(c + (G - 1), quarter(sz_all, c - 1), aux_kt[0])]})
            pieces(N_KV, N_KV, {2: [lambda: silu_z(2 * G - 1, quarter(sz_all, G - 1), aux_kt[0])]})

            def after_v_b(k):
                return {2: [lambda: copy_kT(k)], 4: [lambda: softmax_exp(k, 0)], 5: [lambda: softmax_exp(k, 1)]}

            def after_k_b(k):
                return {0: [lambda: copy_probsT(k, 0)], 1: [lambda: copy_probsT(k, 1)],
                        4: [lambda: gated_hi(k, k - G)]}

            with act.Fori(0, G - 1) as g:
                n = g * (2 * PC) + (N_KV + PC)
                pieces(n, N_KV, after_v_b(g + G))
                pieces(n + PC, N_KV, after_k_b(g + G))
            pieces(N_OUT[1] - PC, N_KV, after_v_b(2 * G - 1))
            out_ple_gate(1, after_k_b(2 * G - 1))

        @block.vector
        def _(dve):
            def split(n, r):
                dve.wait_ge(hi_ready, n + 1)
                nc.vector.tensor_tensor(w_lo[:, r], raw[:, r % RAWS], w_hi[:, r].bitcast(F32), ALU.subtract) \
                    .then_inc(lo_ready, 1)

            def pieces(n, base, after=None, count=PC, before=None):
                for j in range(count):
                    for step in (before or {}).get(j, ()):
                        step()
                    if not isinstance(n, int) or n + j + SPLITS < PIECES:
                        split(n + (j + SPLITS), (base + j) % SPLITS)
                    for step in (after or {}).get(j, ()):
                        step()

            def operand_lo(s, dst, src, c):
                dve.wait_ge(act_hi, s + 1)
                nc.vector.tensor_tensor(quarter(dst[:, 1], c), src, quarter(dst[:, 0], c).bitcast(F32),
                                        ALU.subtract).then_inc(act_ready, 1)

            def evacuate(n_end, parity, dst):
                dve.wait_ge(piece_used, n_end)
                nc.vector.tensor_scalar(dst, acc_of(parity), 1.0, None, ALU.mult).then_inc(chunk_evac, 1)

            def softplus(k, b):
                dve.wait_ge(ln_done, k * 2 + (b + 1))
                nc.vector.scalar_tensor_tensor(out=prob[:, b], in0=scores_of(b), scalar=0.0, in1=prob[:, b],
                                               op0=ALU.max, op1=ALU.add).then_inc(sp_raw, 1)
                dve.wait_ge(sp_raw, k * 2 + (b + 1))
                for h in range(2):
                    diagonal = prob[:, b, h].rearrange("p (s c) -> p s c", c=P)[:, 0:3:2]
                    last = nc.vector.tensor_tensor(diagonal, diagonal,
                                                   past[:, :].unsqueeze(1).broadcast_to((P, 2, P)), ALU.mult)
                last.then_inc(sp_ready, 1)

            def softplus_lo(k, b):
                dve.wait_ge(sp_hi, k * 2 + (b + 1))
                nc.vector.tensor_tensor(sp_parts[:, 1, b], prob[:, b], sp_parts[:, 0, b].bitcast(F32),
                                        ALU.subtract).then_inc(sp_lo, 1)

            def gate_group(k, c, sz):
                dve.wait_ge(sz_ready, k + 1)
                dve.wait_ge(pv_done, k * 2 + 2)
                o = aux[:, :].rearrange("p (b s n) -> p b s n", b=2, s=2)[:, :, 0]
                nc.vector.tensor_tensor(gt.rearrange("p (b h) t -> p b (h t)", b=2), o,
                                        sz.rearrange("p (b h) t -> p b (h t)", b=2), ALU.mult).then_inc(gated, 1)

            def gated_lo(k, c, s):
                operand_lo(s, act1, gt, c)

            for j in range(PC):
                dve.wait_ge(act_hi, j + 1)
                part = slice(PIECE_K * j, PIECE_K * (j + 1))
                nc.vector.tensor_tensor(act0[:, 1, part], x_raw[:, part], act0[:, 0, part].bitcast(F32),
                                        ALU.subtract).then_inc(act_ready, 1)
                split(j, j)

            def chunk_end(n, parity, dst):
                return {PC - 1: [lambda: evacuate(n + PC, parity, dst)]}

            def v_steps(k, n):
                return {5: [lambda: softplus(k, 0)], 6: [lambda: softplus(k, 1)],
                        7: [lambda: softplus_lo(k, 0), lambda: evacuate(n + PC, 0, vn_a)]}

            def z_steps(k, n):
                return {0: [lambda: softplus_lo(k, 1)]} | chunk_end(n, 1, zn_a)

            def gate_steps(k):
                return {2: [lambda: gate_group(k, k, gt)], 3: [lambda: gated_lo(k, k, k + S_OUT[0])]}

            dve.wait_ge(consts_done, 13)
            pieces(0, 0, chunk_end(0, 0, qn))
            pieces(PC, 0, chunk_end(PC, 1, kn))
            with dve.Fori(0, G - 1) as g:
                n = g * (4 * PC) + 2 * PC
                pieces(n, 0, v_steps(g, n))
                pieces(n + PC, 0, z_steps(g, n + PC))
                pieces(n + 2 * PC, 0, gate_steps(g) | chunk_end(n + 2 * PC, 0, qn))
                pieces(n + 3 * PC, 0, chunk_end(n + 3 * PC, 1, kn))
            n = N_OUT[0] - 2 * PC
            pieces(n, 0, v_steps(G - 1, n))
            pieces(n + PC, 0, z_steps(G - 1, n + PC))

            def add_residual(layer, c, used):
                dve.wait_ge(piece_used, N_OUT[layer] + used)
                dve.wait_ge(res_landed[c], 16 * (layer + 1))
                r = columns(res[layer], c)
                nc.vector.scalar_tensor_tensor(out=r, in0=r, scalar=ALPHA, in1=acc_of(c % 2),
                                               op0=ALU.mult, op1=ALU.add).then_inc(chunk_evac, 1)
                dve.wait_ge(chunk_evac, C_OUT[layer] + c + 1)
                statistics(r, c)

            def add_last_residual(layer):
                c = G - 1
                dve.wait_ge(res_landed[c], 16 * (layer + 1))
                r = columns(res[layer], c)
                for t, (done, count, added) in enumerate((
                        (tile_0_done, layer + 1, tile_0_added),
                        (piece_used, N_PLE[layer], chunk_evac))):
                    dve.wait_ge(done, count)
                    nc.vector.scalar_tensor_tensor(out=r[:, t], in0=r[:, t], scalar=ALPHA, in1=acc_of(c % 2)[:, t],
                                                   op0=ALU.mult, op1=ALU.add).then_inc(added, 1)
                    dve.wait_ge(added, layer + 1 if t == 0 else C_OUT[layer] + G)
                    stat = nc.vector.bn_stats(stats[:, t, c, :], r[:, t])
                stat.then_inc(stats_done, 1)

            def statistics(r, c):
                for t in range(TT):
                    s = stats[:, t, c, :] if isinstance(c, int) else stats[:, t, bass.ds(c, 1), :]
                    last = nc.vector.bn_stats(s, r[:, t])
                last.then_inc(stats_done, 1)

            def find_shift(k):
                dve.wait_ge(stats_done, G * (k + 1))
                for t in range(TT):
                    last = nc.vector.bn_aggr(moments[:, t], stats[:, t])
                last.then_inc(moments_done, 1)
                dve.wait_ge(moments_done, k + 1)
                nc.vector.tensor_scalar(var_eps[:, :], moments[:, :, 1], LN_EPS, None, ALU.add).then_inc(var_done, 1)
                dve.wait_ge(rstd_done, k + 1)
                nc.vector.scalar_tensor_tensor(out=shift[:, :], in0=moments[:, :, 0], scalar=-1.0, in1=rstd[:, :],
                                               op0=ALU.mult, op1=ALU.mult).then_inc(shift_done, 1)
                dve.wait_ge(shift_done, k + 1)

            def normalise(src, dst):
                nc.vector.tensor_scalar(dst[:, 0], src[:, 0], rstd[:, 0:1], shift[:, 0:1],
                                        ALU.mult, ALU.add).then_inc(normed_0, 1)

            def full_quarter(k, c, pair, which, s):
                dve.wait_ge(lnT_psum, k + 1)
                dve.wait_ge(act_ready, s)
                for i in range(HG):
                    if isinstance(c, int):
                        g, b = (ln_col[:, which, s, HG * c + i:HG * c + i + 1] for s in range(2))
                    else:
                        g, b = (ln_col[:, which, s, bass.ds(c * HG + i, 1)] for s in range(2))
                    last = nc.vector.tensor_scalar(stage_kt[:, i], aux_kt[pair][:, i], g, b, ALU.mult, ALU.add)
                last.then_inc(full_ready, 1)

            def full_lo(s, c):
                operand_lo(s, act0, stage_kt, c)

            def split_p(layer):
                dve.wait_ge(p_hi, layer + 1)
                nc.vector.tensor_tensor(p_act[:, 1], p_raw, p_act[:, 0].bitcast(F32), ALU.subtract) \
                    .then_inc(p_ready, 1)

            def add_ple(layer, c):
                e = c + layer * G
                r = columns(res[layer], c)
                dve.wait_ge(sig_ready, e + 1)
                dve.wait_ge(ple_evac, G * (layer + 1))
                nc.vector.tensor_tensor(stage_tn, stage_tn, columns(ple[layer], c), ALU.mult).then_inc(chunk_evac, 1)
                dve.wait_ge(chunk_evac, c + (C_GATE[layer] + 1))
                dve.wait_ge(x1_ready, e + 1)
                if layer:
                    nc.vector.tensor_tensor(r, r, stage_tn, ALU.add).then_inc(x2_ready, 1)
                else:
                    nc.vector.tensor_tensor(stage_tn, r, stage_tn, ALU.add).then_inc(x2_sum, 1)
                    dve.wait_ge(x2_sum, e + 1)
                    nc.vector.tensor_scalar(r, stage_tn, 1.0, None, ALU.mult).then_inc(x2_ready, 1)
                    statistics(stage_tn, c)

            def x2_lo(c):
                operand_lo(c + S_X2, act1, aux_kt[0], c)

            def out_ple_gate(layer, after_out):
                n = N_OUT[layer]
                s = S_GATE[layer]
                k = 2 * G * layer
                ends = {OUT_ORDER.index((c, PC - 1)): c for c in range(G)}
                x1 = [columns(res[layer], c) for c in range(G)]
                turned = [[lambda c=c: full_quarter(k + c, c, c % 2, layer, s + c), lambda c=c: full_lo(s + c, c)]
                          for c in range(G)]
                pieces(n, n, after_out | {12: [lambda: split_p(layer)]}, G * PC,
                       before={i: [lambda c=c, i=i: add_residual(layer, c, i + 1)] for i, c in ends.items()
                               if c < G - 1}
                       | {G * PC - 1: [lambda: add_last_residual(layer), lambda: find_shift(2 * layer)]
                          + [lambda r=r: normalise(r, r) for r in x1] + turned[0]})
                pieces(N_PLE[layer], N_PLE[layer], count=G,
                       before={0: turned[1], 2: turned[2]})
                n = N_GATE[layer]
                pieces(n, n, {PC - 1: [lambda: add_ple(layer, 0)]}, before={0: turned[3]})
                with dve.Fori(1, G - layer) as c:
                    pieces(c * PC + n, n, ({3: [lambda: x2_lo(c - 1)]} if layer == 0 else {})
                           | {PC - 1: [lambda: add_ple(layer, c)]})
                if layer:
                    c = G - 1
                    dve.wait_ge(ple_evac, 2 * G)
                    dve.wait_ge(x1_ready, 2 * G)
                    for t in range(TT):
                        r, gate = columns(res[1], c)[:, t], stage_tn[:, t]
                        dve.wait_ge(sig_ready, 2 * G + t)
                        nc.vector.tensor_tensor(gate, gate, columns(ple[1], c)[:, t], ALU.mult) \
                            .then_inc(chunk_evac, 1)
                        dve.wait_ge(chunk_evac, C_GATE[1] + G + t)
                        nc.vector.tensor_tensor(r, r, gate, ALU.add).then_inc(x2_ready, 1)

            out_ple_gate(0, gate_steps(G - 1))

            def rotate(n_end, parity):
                dve.wait_ge(piece_used, n_end)
                src = acc_of(parity).rearrange("p t (h d) -> p t h d", d=DH)
                first, second = src[:, :, :, 0:HALF], src[:, :, :, HALF:DH]
                cos, sin = (cos_sin[:, i].unsqueeze(2).broadcast_to((P, TT, HG, HALF)) for i in range(2))
                nc.vector.tensor_tensor(roped_out[:, :, :, 0:HALF], first, cos, ALU.mult)
                nc.vector.tensor_tensor(roped_out[:, :, :, HALF:DH], second, cos, ALU.mult)
                nc.vector.tensor_tensor(rope_tmp[:, :, :, 0:HALF], second, sin, ALU.mult).then_inc(rope_mul, 1)
                nc.vector.tensor_tensor(rope_tmp[:, :, :, HALF:DH], first, sin, ALU.mult).then_inc(chunk_evac, 1)

            def rotate_end(k, c_evac):
                dve.wait_ge(rope_mul, k + 1)
                dve.wait_ge(chunk_evac, c_evac)
                nc.vector.tensor_tensor(roped_out[:, :, :, 0:HALF], roped_out[:, :, :, 0:HALF],
                                        rope_tmp[:, :, :, 0:HALF], ALU.subtract)
                nc.vector.tensor_tensor(roped_out[:, :, :, HALF:DH], roped_out[:, :, :, HALF:DH],
                                        rope_tmp[:, :, :, HALF:DH], ALU.add).then_inc(roped, 1)

            def q_end(c, parity):
                return {PC - 1: [lambda: rotate(c * PC + (N_Q + PC), parity),
                                 lambda: rotate_end(c, c + (C_Q + 1))]}

            def normalise_x2(c):
                normalise(columns(res[0], c), v_or_z)

            def ln_quarter(c):
                return [lambda: full_quarter(c + G, c, 1, 2, c + S_KV), lambda: full_lo(c + S_KV, c)]

            dve.wait_ge(tables_landed, 32)
            pieces(N_Q, N_Q, {2: [lambda: x2_lo(G - 1), lambda: find_shift(1), lambda: normalise_x2(0)],
                               6: ln_quarter(0)} | q_end(0, 0))
            with dve.Fori(1, G) as c:
                pieces(c * PC + N_Q, N_Q, {3: [lambda: normalise_x2(c)], 5: ln_quarter(c)} | q_end(c, c % 2))
            pieces(N_Z, N_Z, chunk_end(N_Z, 0, v_or_z[:, :, :]))
            with dve.Fori(1, G) as c:
                n = c * PC + N_Z
                pieces(n, N_Z, chunk_end(n, c % 2, v_or_z[:, :, :]))

            def k_end(n, g):
                return {PC - 1: [lambda: rotate(n + PC, 0),
                                 lambda: rotate_end(g + G, g * 2 + (C_KV + 1))]}

            def row_max(k, b):
                dve.wait_ge(scores_ready, k * 2 + (b + 1))
                for t, (lo, hi) in enumerate(((0, P), (P, SC))):
                    last = nc.vector.tensor_reduce(out=neg_max[:, b, 2 * t:2 * t + 2],
                                                   in_=aux_b[:, 2 * b:2 * b + 2, lo:hi],
                                                   axis=AX.X, op=ALU.max, negate=True)
                last.then_inc(neg_max_ready, 1)

            def divide(k, b):
                i = (k - G) * 2 + (b + 1)
                dve.wait_ge(probs_raw, i)
                nc.vector.reciprocal(row_sum[:, b], row_sum[:, b]).then_inc(inv_ready, 1)
                dve.wait_ge(inv_ready, i)
                for t, (lo, hi) in enumerate(((0, P), (P, SC))):
                    part = prob[:, b, :, lo:hi]
                    last = nc.vector.tensor_tensor(
                        part, part, row_sum[:, b, 2 * t:2 * t + 2].unsqueeze(2).broadcast_to((P, 2, hi - lo)),
                        ALU.mult)
                last.then_inc(probs_ready, 1)

            def after_v_b(k):
                return {4: [lambda: row_max(k, 0)], 5: [lambda: row_max(k, 1), lambda: divide(k, 0)],
                        6: [lambda: divide(k, 1)]}

            def after_k_b(k):
                return {4: [lambda: gate_group(k, k - G, quarter(sz_all, k - G)),
                            lambda: gated_lo(k, k - G, (k - G) + S_OUT[1])]}

            pieces(N_KV, N_KV, k_end(N_KV, 0))
            with dve.Fori(0, G - 1) as g:
                n = g * (2 * PC) + (N_KV + PC)
                pieces(n, N_KV, after_v_b(g + G) | chunk_end(n, 1, v_or_z[:, :, :]))
                pieces(n + PC, N_KV, after_k_b(g + G) | k_end(n + PC, g + 1))
            n = N_OUT[1] - PC
            pieces(n, N_KV, after_v_b(2 * G - 1) | chunk_end(n, 1, v_or_z[:, :, :]))
            out_ple_gate(1, after_k_b(2 * G - 1))

        @block.tensor
        def _(pe):
            def piece(n, r, operand, tiles, out_banks, first, final, by_token=False):
                pe.wait_ge(lo_ready, n + 1)
                order = [(i, t) for i in range(PIECE_K) for t in range(TT)]
                for i, t in sorted(order, key=lambda it: it[1]) if by_token else order:
                    hi, lo = (operand[:, s, tiles[i], t * P:(t + 1) * P] for s in range(2))
                    dst = out_banks[:, t]
                    begin, end = first and i == 0, final and i == PIECE_K - 1
                    nc.tensor.matmul(dst, hi, w_hi[:, r, i], start=begin, stop=False)
                    nc.tensor.matmul(dst, hi, w_lo[:, r, i], start=False, stop=False)
                    mm = nc.tensor.matmul(dst, lo, w_hi[:, r, i], start=False, stop=end)
                    if by_token and t == 0 and end:
                        mm.then_inc(tile_0_done, 1)
                mm.then_inc(piece_used, 1)

            def chunk(n, base, operand, parity, c, quarters=None, after=None, last=False):
                if not isinstance(c, int) or c >= 2:
                    pe.wait_ge(chunk_evac, c - 1)
                for j in range(PC):
                    if quarters == S_X:
                        pe.wait_ge(act_ready, j + 1)
                    elif quarters is not None and j % 2 == 0:
                        pe.wait_ge(act_ready, quarters + j // 2 + 1)
                    piece(n + j, (base + j) % SPLITS, operand, range(PIECE_K * j, PIECE_K * (j + 1)),
                          acc_of(parity), j == 0, j == PC - 1, by_token=last and j == PC - 1)
                    for step in (after or {}).get(j, ()):
                        step()

            def transposes(src, dst, signal):
                for i in range(HG):
                    for t in range(TT):
                        mm = nc.tensor.transpose(dst[:, i, t * P:(t + 1) * P], src[:, t, i * P:(i + 1) * P],
                                                 ident[:, :])
                mm.then_inc(signal, 1)

            def q_turn(k, c):
                pe.wait_ge(chunk_evac, c + 1)
                if not isinstance(k, int) or k > 0:
                    pe.wait_ge(gated, k)
                transposes(qn, aux_kt[0], qT_psum)

            def k_turn(k, c):
                pe.wait_ge(chunk_evac, c + 1)
                transposes(kn, aux_kt[1], kT_psum)

            def key_scores(k, b):
                pe.wait_ge(qT_ready, k + 1)
                pe.wait_ge(kT_ready, k + 1)
                for h in (2 * b, 2 * b + 1):
                    s = aux_b[:, h]
                    nc.tensor.matmul(s[:, 0:T], kT[:, h, 0:P], qT[:, h, :], start=True, stop=True,
                                     skip_group_check=True)
                    mm = nc.tensor.matmul(s[:, T:SC], kT[:, h, P:T], qT[:, h, P:T], start=False, stop=True,
                                          skip_group_check=True)
                mm.then_inc(scores_ready, 1)

            def cumulate(k, b):
                pe.wait_ge(sp_lo, k * 2 + (b + 1))
                for i, h in enumerate((2 * b, 2 * b + 1)):
                    s, (hi, lo) = aux_b[:, h], (sp_parts[:, part, b, i] for part in range(2))
                    for dst, lhs, rhs in ((s[:, 0:SC], neg_upper, hi), (s[:, 0:SC], neg_upper, lo),
                                          (s[:, P:T], neg_ones, hi[:, T:SC]), (s[:, P:T], neg_ones, lo[:, T:SC]),
                                          (s[:, 0:P], ident16, not_past[:, :]),
                                          (s[:, T:SC], ident16, not_past[:, :])):
                        mm = nc.tensor.matmul(dst, lhs[:, :], rhs, start=False, stop=True,
                                              skip_group_check=True)
                mm.then_inc(cum_ready, 1)

            def weigh_values(k, b, v, v_chunk):
                pe.wait_ge(w_ready, k * 2 + (b + 1))
                pe.wait_ge(chunk_evac, v_chunk + 1)
                for i in range(2):
                    head = slice((2 * b + i) * P, (2 * b + i + 1) * P)
                    o, w = aux_b[:, 2 * b, i * T:(i + 1) * T], prob[:, b, i]
                    nc.tensor.matmul(o, v[:, 0, head], w[:, 0:T], start=(i == 0), stop=True,
                                     skip_group_check=True)
                    mm = nc.tensor.matmul(o[:, P:T], v[:, 1, head], w[:, T:SC], start=False, stop=True,
                                          skip_group_check=True)
                mm.then_inc(pv_done, 1)

            def z_turn(k, c):
                pe.wait_ge(chunk_evac, c + 1)
                for i in range(HG):
                    for t in range(TT):
                        bank = aux_b[:, 2 * (i // 2) + 1]
                        at = (i % 2) * T + t * P
                        mm = nc.tensor.transpose(bank[:, at:at + P], zn_a[:, t, i * P:(i + 1) * P], ident[:, :])
                mm.then_inc(zT_psum, 1)

            def after_k(k, c):
                return {4: [lambda: q_turn(k, c - 1)]}

            def after_v(k, c):
                return {2: [lambda: k_turn(k, c - 1)], 4: [lambda: key_scores(k, 0)],
                        5: [lambda: key_scores(k, 1)]}

            def after_z(k, c):
                return {2: [lambda: cumulate(k, 0)], 3: [lambda: cumulate(k, 1)],
                        6: [lambda: weigh_values(k, 0, vn_a, c - 1)],
                        7: [lambda: weigh_values(k, 1, vn_a, c - 1)]}

            def z_step(k, c):
                return {2: [lambda: z_turn(k, c)]}

            pe.wait_ge(consts_done, 3)
            for _ in range(WARM_UPS):
                nc.tensor.matmul(aux[:, 0:P], neg_ones_raw, neg_ones_raw, start=True, stop=True)
            pe.wait_ge(consts_done, 13)
            chunk(0, 0, act0, 0, 0, quarters=S_X)
            chunk(PC, 0, act0, 1, 1, after=after_k(0, 1))
            pe.wait_ge(masks_done, 1)
            with pe.Fori(0, G - 1) as g:
                n = g * (4 * PC) + 2 * PC
                c = g * 4 + 2
                chunk(n, 0, act0, 0, c, after=after_v(g, c))
                chunk(n + PC, 0, act0, 1, c + 1, after=after_z(g, c + 1))
                chunk(n + 2 * PC, 0, act0, 0, c + 2, after=z_step(g, c + 1))
                chunk(n + 3 * PC, 0, act0, 1, c + 3, after=after_k(g + 1, c + 3))
            c = C_OUT[0] - 2
            chunk(c * PC, 0, act0, 0, c, after=after_v(G - 1, c))
            chunk((c + 1) * PC, 0, act0, 1, c + 1, after=after_z(G - 1, c + 1))

            def ln_turn(k, c, pair, layer, src):
                pe.wait_ge(normed_0, k + 1)
                pe.wait_ge(normed_1, k + 1)
                transposes(src if c is None else columns(src, c), aux_kt[pair], lnT_psum)

            def out_projection(layer, after_out):
                for i, (c, j) in enumerate(OUT_ORDER):
                    n = N_OUT[layer] + i
                    if j == 0:
                        pe.wait_ge(chunk_evac, C_OUT[layer] + c - 1)
                    if c == 0 and j % 2 == 0:
                        pe.wait_ge(act_ready, S_OUT[layer] + j // 2 + 1)
                    piece(n, n % SPLITS, act1, range(PIECE_K * j, PIECE_K * (j + 1)), acc_of(c % 2),
                          j == 0, j == PC - 1, by_token=i == G * PC - 1)
                    for step in after_out.get(i, ()):
                        step()

            def ple_and_gate(layer):
                k = 2 * G * layer
                s = S_GATE[layer]

                def turn(i):
                    if i < 2:
                        pe.wait_ge(ple_evac, layer * G + i + 1)
                    else:
                        pe.wait_ge(full_ready, k + i - 1)
                    ln_turn(k + i, i, i % 2, layer, res[layer])

                pe.wait_ge(p_ready, layer + 1)
                for c in range(G):
                    n = N_PLE[layer] + c
                    if c >= 2:
                        pe.wait_ge(chunk_evac, C_OUT[layer] + c + 1)
                    banks = acc_of(c % 2) if c >= 2 else \
                        aux[:, c * 2 * COLS:(c + 1) * 2 * COLS].rearrange(tokens, t=TT)
                    piece(n, n % SPLITS, act0, range(KT - PIECE_K, KT), banks, True, True)
                    if c >= 1:
                        turn(c - 1)
                n, c0 = N_GATE[layer], C_GATE[layer]
                pe.wait_ge(ple_evac, layer * G + G - 1)
                chunk(n, n, act0, 0, c0, quarters=s, after={1: [lambda: turn(3)]})
                pe.wait_ge(ple_evac, layer * G + G)
                with pe.Fori(1, G - layer) as c:
                    chunk(c * PC + n, n, act0, c % 2, c + c0,
                          after={3: [lambda: x2_turn(c - 1)]} if layer == 0 else None)
                if layer:
                    c = G - 1
                    chunk(c * PC + n, n, act0, c % 2, c + c0, last=True)

            def x2_turn(c):
                pe.wait_ge(x2_ready, c + 1)
                pe.wait_ge(act_ready, c + S_X2)
                transposes(stage_tn, aux_kt[0], x2T_psum)

            out_projection(0, z_step(G - 1, C_OUT[0] - 1))
            ple_and_gate(0)

            def ln_step(c):
                if not isinstance(c, int):
                    pe.wait_ge(full_ready, c + G)
                ln_turn(c + G, None, 1, 0, v_or_z)

            def q_turn_b(c):
                pe.wait_ge(roped, c + 1)
                if isinstance(c, int) and c == 0:
                    pe.wait_ge(act_ready, S_X2 + G)
                else:
                    pe.wait_ge(qT_ready, c + G)
                transposes(roped_rows, aux_kt[0], qT_psum)

            def z_turn_b(c):
                pe.wait_ge(chunk_evac, c + (C_Z + 1))
                pe.wait_ge(sz_ready, c + G)
                transposes(v_or_z, aux_kt[0], zT_psum)

            def k_turn_b(k):
                pe.wait_ge(roped, k + 1)
                pe.wait_ge(gated, k)
                transposes(roped_rows, aux_kt[1], kT_psum)

            def query_scores(k, b):
                pe.wait_ge(kT_ready, k + 1)
                pe.wait_ge(q_group_ready, (k - G) + 1)
                for h in (2 * b, 2 * b + 1):
                    s, first = aux_b[:, h], True
                    for dst, lhs, rhs in ((s[:, 0:P], qT[:, h, 0:P], kT[:, h, 0:P]),
                                          (s[:, P:SC], qT[:, h, P:T], kT[:, h, :]),
                                          (s[:, 0:P], ident16[:, :], future[:, :]),
                                          (s[:, T:SC], ident16[:, :], future[:, :])):
                        mm = nc.tensor.matmul(dst, lhs, rhs, start=first, stop=True, skip_group_check=True)
                        first = False
                mm.then_inc(scores_ready, 1)

            def probs_turn(k, b):
                pe.wait_ge(probs_ready, (k - G) * 2 + (b + 1))
                for i in range(2):
                    for s in range(3):
                        mm = nc.tensor.transpose(aux_b[:, 2 * b + i, s * P:(s + 1) * P],
                                                 prob[:, b, i, s * P:(s + 1) * P], ident[:, :])
                mm.then_inc(probsT_psum, 1)

            chunk(N_Q, N_Q, act1, 0, C_Q, quarters=S_X2,
                  after={2: [lambda: x2_turn(G - 1)], 6: [lambda: ln_step(0)]})
            with pe.Fori(1, G) as c:
                chunk(c * PC + N_Q, N_Q, act1, c % 2, c + C_Q,
                      after={2: [lambda: q_turn_b(c - 1)], 5: [lambda: ln_step(c)]})
            chunk(N_Z, N_Z, act1, 0, C_Z, after={2: [lambda: q_turn_b(G - 1)]})
            with pe.Fori(1, G) as c:
                chunk(c * PC + N_Z, N_Z, act1, c % 2, c + C_Z, after={2: [lambda: z_turn_b(c - 1)]})

            def after_v_b(k):
                return {2: [lambda: k_turn_b(k)], 4: [lambda: query_scores(k, 0)],
                        5: [lambda: query_scores(k, 1)]}

            def after_k_b(k, v_chunk):
                v = v_or_z
                return {0: [lambda: probs_turn(k, 0)], 1: [lambda: probs_turn(k, 1)],
                        3: [lambda: weigh_values(k, 0, v, v_chunk)],
                        4: [lambda: weigh_values(k, 1, v, v_chunk)]}

            chunk(N_KV, N_KV, act0, 0, C_KV, quarters=S_KV, after={2: [lambda: z_turn_b(G - 1)]})
            pe.wait_ge(sz_ready, 2 * G)
            with pe.Fori(0, G - 1) as g:
                n = g * (2 * PC) + (N_KV + PC)
                c = g * 2 + (C_KV + 1)
                chunk(n, N_KV, act0, 1, c, after=after_v_b(g + G))
                chunk(n + PC, N_KV, act0, 0, c + 1, after=after_k_b(g + G, c))
            c = C_OUT[1] - 1
            chunk(N_OUT[1] - PC, N_KV, act0, 1, c, after=after_v_b(2 * G - 1))
            out_projection(1, after_k_b(2 * G - 1, c))
            ple_and_gate(1)


def kernel(x, p, w_in_a, w_out_a, w_kv, ln_kv_g, ln_kv_b, w_in_b, w_out_b, ln_g, ln_b, w_ple, w_ple_gate):
    import concourse.bacc as bacc
    from concourse.bass_utils import run_bass_kernel_spmd

    x, p, ln_g, ln_b, ln_kv_g, ln_kv_b = (np.asarray(a) for a in (x, p, ln_g, ln_b, ln_kv_g, ln_kv_b))
    depth, _, seq, d = p.shape[0], p.shape[1], x.shape[1], x.shape[2]
    tiles = d // P
    half = P // 2
    inv_freq = np.float32(10000.0) ** (-np.arange(half, dtype=np.float32) / np.float32(half))
    angle = np.arange(seq, dtype=np.float32)[:, None] * inv_freq[None, :]
    rope = np.stack([np.cos(angle), np.sin(angle)]).astype(np.float32)
    by_feature = np.stack([np.stack([ln_g[0], ln_b[0]]), np.stack([ln_g[1], ln_b[1]]),
                           np.stack([ln_kv_g, ln_kv_b])])
    arrays = {
        "xt": np.ascontiguousarray(x[0].T),
        "x": np.ascontiguousarray(x[0]),
        "pt": np.ascontiguousarray(p[:, 0].transpose(0, 2, 1)),
        "w_in_a": np.asarray(w_in_a), "w_out_a": np.asarray(w_out_a), "w_kv": np.asarray(w_kv),
        "w_in_b": np.asarray(w_in_b), "w_out_b": np.asarray(w_out_b), "w_ple": np.asarray(w_ple),
        "w_ple_gate": np.asarray(w_ple_gate),
        "ln_rows": np.ascontiguousarray(np.stack([ln_g, ln_b], axis=1)),
        "ln_cols": np.ascontiguousarray(by_feature.reshape(3, 2, tiles, P).transpose(3, 0, 1, 2)),
        "rope": np.ascontiguousarray(rope.reshape(2, seq // P, P, half).transpose(2, 0, 1, 3)),
    }
    assert depth == 2
    nc = bacc.Bacc("TRN2", target_bir_lowering=False, num_devices=1)
    args = [nc.dram_tensor(f"in_{n}", a.shape, mybir.dt.from_np(a.dtype), kind="ExternalInput").ap()
            for n, a in arrays.items()]
    out = nc.dram_tensor("out", (seq, d), F32, kind="ExternalOutput").ap()
    build(nc, *args, out)
    r = run_bass_kernel_spmd(nc, [{f"in_{n}": a for n, a in arrays.items()}], core_ids=[0])
    return np.asarray(r.results[0]["out"]).reshape(1, seq, d)
```

```python
import math
from contextlib import ExitStack

import concourse.bass as bass
import numpy as np
from concourse import mybir

F32 = mybir.dt.float32
F32R = mybir.dt.float32r
BF16 = mybir.dt.bfloat16
ALU = mybir.AluOpType
ACT = mybir.ActivationFunctionType
AX = mybir.AxisListType

P = 128
NEG = -1e30
LN_EPS = 1e-5
COLS = 512
PIECE_K = 2
RAWS = 4
SPLITS = 8
WARM_UPS = 14


def build(nc, xt, x, pt, w_in_a, w_out_a, w_kv, w_in_b, w_out_b, w_ple, w_ple_gate,
          ln_rows, ln_cols, rope, out):
    D, T = xt.shape
    TT = T // P
    KT = D // P
    DH = P
    HG = COLS // DH
    G = D // COLS
    PC = KT // PIECE_K
    HALF = DH // 2
    LAYERS = w_ple.shape[0]
    ALPHA = (2.0 * LAYERS) ** 0.25
    SCALE = 1.0 / math.sqrt(DH)
    SC = 3 * P
    assert TT == 2 and PC == SPLITS and LAYERS == 2 and HG == 4 and G == 4

    N_QKVZ = 0
    N_OUT = [N_QKVZ + 4 * G * PC, 0]
    N_PLE = [N_OUT[0] + G * PC, 0]
    N_GATE = [N_PLE[0] + G, 0]
    N_Q = N_GATE[0] + G * PC
    N_Z = N_Q + G * PC
    N_KV = N_Z + G * PC
    N_OUT[1] = N_KV + 2 * G * PC
    N_PLE[1] = N_OUT[1] + G * PC
    N_GATE[1] = N_PLE[1] + G
    PIECES = N_GATE[1] + G * PC
    C_QKVZ = 0
    C_OUT = [C_QKVZ + 4 * G, 0]
    C_GATE = [C_OUT[0] + G, 0]
    C_Q = C_GATE[0] + G
    C_Z = C_Q + G
    C_KV = C_Z + G
    C_OUT[1] = C_KV + 2 * G
    C_GATE[1] = C_OUT[1] + G
    S_X = 0
    S_OUT = [PC, PC + 4 * G]
    S_GATE = [PC + G, PC + 5 * G]
    S_X2 = PC + 2 * G
    S_KV = PC + 3 * G
    FIRST_ROWS = PC - PIECE_K
    OUT_ORDER = ([(c, j) for c in (0, 1) for j in range(FIRST_ROWS)]
                 + [(c, j) for c in (0, 1) for j in range(FIRST_ROWS, PC)]
                 + [(c, j) for c in range(2, G) for j in range(PC)])

    with ExitStack() as ctx:
        def sb(name, shape, dt=F32):
            return ctx.enter_context(nc.sbuf_tensor(name, [P, *shape], dt))

        def sem(name):
            return ctx.enter_context(nc.semaphore(name))

        raw = sb("raw", [RAWS, PIECE_K, COLS])
        w_hi = sb("w_hi", [SPLITS, PIECE_K, COLS], F32R)
        w_lo = sb("w_lo", [SPLITS, PIECE_K, COLS], F32R)
        act0 = sb("act0", [2, KT, T], F32R)
        act1 = sb("act1", [2, KT, T], F32R)
        big0 = sb("big0", [TT * D])
        big1_at = nc.sbuf_base
        big1 = sb("big1", [TT * D])
        q_parts = nc.alloc_sbuf_tensor_at("q_parts", [P, 2, HG, T], F32R, offset=big1_at)
        k_parts = nc.alloc_sbuf_tensor_at("k_parts", [P, 2, HG, P], F32R, offset=big1_at + 4 * 2 * HG * T)
        sp_parts = nc.alloc_sbuf_tensor_at("sp_parts", [P, 2, 2, 2, SC], F32R, offset=big1_at)
        w_parts = nc.alloc_sbuf_tensor_at("w_parts", [P, 2, 2, 2, T], F32R, offset=big1_at)
        heads = sb("heads", [3 * HG * T + 2 * 2 * SC])
        v_or_z_at = nc.sbuf_base
        v_or_z = sb("v_or_z", [TT, COLS])
        v_parts = nc.alloc_sbuf_tensor_at("v_parts", [P, 2, COLS], F32R, offset=v_or_z_at)
        stage_at = nc.sbuf_base
        stage = sb("stage", [HG * T])
        q1_parts = nc.alloc_sbuf_tensor_at("q1_parts", [P, 2, HG, P], F32R, offset=stage_at)
        v1_parts = nc.alloc_sbuf_tensor_at("v1_parts", [P, 2, COLS], F32R, offset=stage_at)
        ident = sb("ident", [P])
        neg_upper = sb("neg_upper", [P], F32R)
        neg_ones = sb("neg_ones", [P], F32R)
        past = sb("past", [P])
        not_past = sb("not_past", [P], BF16)
        future = sb("future", [P], BF16)
        cos_sin = sb("cos_sin", [2, TT, HALF])
        ln_col = sb("ln_col", [3, 2, KT])
        stats = sb("stats", [TT, G, 6])
        moments = sb("moments", [TT, 2])
        var_eps = sb("var_eps", [TT])
        minus_half = sb("minus_half", [TT])
        rstd = sb("rstd", [TT])
        shift = sb("shift", [TT])
        neg_max = sb("neg_max", [2, 2 * TT])
        row_sum = sb("row_sum", [2, 2 * TT])
        acc = ctx.enter_context(nc.psum_tensor("acc", [P, 4 * COLS], F32))
        aux = ctx.enter_context(nc.psum_tensor("aux", [P, 4 * COLS], F32))
        x2_spill = nc.dram_tensor("x2_spill", [T, D], F32).ap()

        tokens = "p (t n) -> p t n"
        qn, kn, vn_a, zn_a = (big0[:, i * TT * COLS:(i + 1) * TT * COLS].rearrange(tokens, t=TT)
                              for i in range(4))
        q_all = big0[:, :].rearrange("p (h t) -> p h t", t=T)
        sz_all = big1[:, :].rearrange("p (h t) -> p h t", t=T)
        x_raw = big1[:, :].rearrange("p (k t) -> p k t", t=T)
        res = [big1[:, :].rearrange(tokens, t=TT), big0[:, :].rearrange(tokens, t=TT)]
        ple = [big0[:, :].rearrange(tokens, t=TT), big1[:, :].rearrange(tokens, t=TT)]
        HT = HG * T
        kT = heads[:, 0:HT].rearrange("p (h t) -> p h t", t=T)
        qT = heads[:, HT:2 * HT].rearrange("p (h t) -> p h t", t=T)
        prob = heads[:, 2 * HT:2 * HT + 4 * SC].rearrange("p (b h c) -> p b h c", b=2, c=SC)
        gt = heads[:, 2 * HT + 4 * SC:].rearrange("p (h t) -> p h t", t=T)
        gain = heads[:, 0:D]
        offset = heads[:, D:2 * D]
        rope_tmp = heads[:, 0:HT].rearrange("p (t h d) -> p t h d", t=TT, d=DH)
        roped_out = heads[:, 2 * HT:3 * HT].rearrange("p (t h d) -> p t h d", t=TT, d=DH)
        roped_rows = heads[:, 2 * HT:3 * HT].rearrange(tokens, t=TT)
        stage_kt = stage[:, :].rearrange("p (k t) -> p k t", t=T)
        stage_tn = stage[:, :].rearrange(tokens, t=TT)
        p_raw = stage[:, 0:PIECE_K * T].rearrange("p (k t) -> p k t", t=T)
        neg_upper_raw, neg_ones_raw = stage[:, 0:P], stage[:, P:2 * P]
        k1_parts = act1[:, :, KT - HG:KT, :]
        w1_parts = k1_parts.rearrange("p s (b h) t -> p s b h t", b=2)
        p_act = act0[:, :, KT - PIECE_K:KT, :]
        aux_b = aux[:, :].rearrange("p (b n) -> p b n", n=COLS)
        aux_kt = [aux[:, 0:HT].rearrange("p (k t) -> p k t", t=T),
                  aux[:, HT:2 * HT].rearrange("p (k t) -> p k t", t=T)]

        def acc_of(parity):
            if isinstance(parity, int):
                return acc[:, parity * 2 * COLS:(parity + 1) * 2 * COLS].rearrange(tokens, t=TT)
            return acc[:, bass.ts(parity, 2 * COLS)].rearrange(tokens, t=TT)

        def quarter(ap, c):
            return ap[:, HG * c:HG * c + HG] if isinstance(c, int) else ap[:, bass.ds(c * HG, HG)]

        def columns(ap, c):
            return ap[:, :, COLS * c:COLS * c + COLS] if isinstance(c, int) else ap[:, :, bass.ts(c, COLS)]

        def scores_of(b):
            return aux_b[:, 2 * b:2 * b + 2, 0:SC]

        w_landed = [sem(f"dma_w_landed{i}") for i in range(RAWS)]
        x_landed = [sem(f"dma_x_landed{i}") for i in range(PC)]
        tables_landed = sem("dma_tables_landed")
        res_landed = [sem(f"dma_res_landed{i}") for i in range(G)]
        p_landed = sem("dma_p_landed")
        ln_rows_landed = sem("dma_ln_rows_landed")
        x2_spilled = sem("dma_x2_spilled")
        out_stored = sem("dma_out_stored")
        consts_done = sem("pool_consts_done")
        rstd_done = sem("pool_rstd_done")
        gained = sem("pool_gained")
        x1_ready = sem("pool_x1_ready")
        q_group_ready = sem("pool_q_group_ready")
        masks_done = sem("act_masks_done")
        hi_ready = sem("act_hi_ready")
        act_hi = sem("act_operand_hi")
        p_hi = sem("act_p_hi")
        qT_ready = sem("act_qT_ready")
        kT_ready = sem("act_kT_ready")
        abs_done = sem("act_abs_done")
        exp_done = sem("act_exp_done")
        ln_done = sem("act_ln_done")
        probs_raw = sem("act_probs_raw")
        w_ready = sem("act_w_ready")
        sp_hi = sem("act_sp_hi")
        q_hi = sem("act_q_hi")
        k_hi = sem("act_k_hi")
        v_hi = sem("act_v_hi")
        weights_hi = sem("act_weights_hi")
        sz_ready = sem("act_sz_ready")
        ple_evac = sem("act_ple_evac")
        sig_ready = sem("act_sig_ready")
        normed_1 = sem("act_normed_1")
        lo_ready = sem("dve_lo_ready")
        act_ready = sem("dve_operand_ready")
        p_ready = sem("dve_p_ready")
        chunk_evac = sem("dve_chunk_evac")
        tile_0_added = sem("dve_tile_0_added")
        masked = sem("dve_masked")
        sp_raw = sem("dve_sp_raw")
        sp_ready = sem("dve_sp_ready")
        sp_lo = sem("dve_sp_lo")
        q_lo = sem("dve_q_lo")
        k_lo = sem("dve_k_lo")
        v_lo = sem("dve_v_lo")
        weights_lo = sem("dve_weights_lo")
        gated = sem("dve_gated")
        rope_mul = sem("dve_rope_mul")
        roped = sem("dve_roped")
        neg_max_ready = sem("dve_neg_max_ready")
        inv_ready = sem("dve_inv_ready")
        probs_ready = sem("dve_probs_ready")
        stats_done = sem("dve_stats_done")
        moments_done = sem("dve_moments_done")
        var_done = sem("dve_var_done")
        shift_done = sem("dve_shift_done")
        normed_0 = sem("dve_normed_0")
        full_ready = sem("dve_full_ready")
        x2_sum = sem("dve_x2_sum")
        x2_ready = sem("dve_x2_ready")
        piece_used = sem("pe_piece_used")
        tile_0_done = sem("pe_tile_0_done")
        qT_psum = sem("pe_qT_psum")
        kT_psum = sem("pe_kT_psum")
        scores_ready = sem("pe_scores_ready")
        cum_ready = sem("pe_cum_ready")
        probsT_psum = sem("pe_probsT_psum")
        pv_done = sem("pe_pv_done")
        zT_psum = sem("pe_zT_psum")
        lnT_psum = sem("pe_lnT_psum")
        x2T_psum = sem("pe_x2T_psum")

        block = ctx.enter_context(nc.Block())

        @block.sync
        def _(sp):
            def load(n, r, matrix, j, c):
                rows = matrix[j * PIECE_K * P:(j + 1) * PIECE_K * P, :]
                cols = rows[:, c * COLS:(c + 1) * COLS] if isinstance(c, int) else rows[:, bass.ts(c, COLS)]
                if not isinstance(n, int) or n >= RAWS:
                    sp.wait_ge(lo_ready, n - RAWS + 1)
                sp.dma_start(raw[:, r % RAWS], cols.rearrange("(k p) n -> p k n", p=P)) \
                    .then_inc(w_landed[r % RAWS], 16)

            def load_chunk(n, base, matrix, c):
                for j in range(PC):
                    load(n + j, (base + j) % SPLITS, matrix, j, c)

            wa = w_in_a[0]
            for j in range(PC):
                sp.dma_start(x_raw[:, PIECE_K * j:PIECE_K * (j + 1), :],
                             xt[j * PIECE_K * P:(j + 1) * PIECE_K * P, :].rearrange("(k p) t -> p k t", p=P)) \
                    .then_inc(x_landed[j], 16)
                load(j, j, wa, j, 0)
            load_chunk(PC, 0, wa, G)
            with sp.Fori(0, G - 1) as g:
                n = g * (4 * PC) + 2 * PC
                load_chunk(n, 0, wa, g + 2 * G)
                load_chunk(n + PC, 0, wa, g + 3 * G)
                load_chunk(n + 2 * PC, 0, wa, g + 1)
                load_chunk(n + 3 * PC, 0, wa, g + 1 + G)
            load_chunk(N_OUT[0] - 2 * PC, 0, wa, 3 * G - 1)
            load_chunk(N_OUT[0] - PC, 0, wa, 4 * G - 1)

            def load_out_ple_gate(layer, w_out):
                n = N_OUT[layer]
                for i, (c, j) in enumerate(OUT_ORDER):
                    load(n + i, (n + i) % SPLITS, w_out, j, c)
                for c in range(G):
                    load(N_PLE[layer] + c, (N_PLE[layer] + c) % SPLITS, w_ple[layer], 0, c)
                with sp.Fori(0, G) as c:
                    load_chunk(c * PC + N_GATE[layer], N_GATE[layer], w_ple_gate[layer], c)

            load_out_ple_gate(0, w_out_a[0])
            with sp.Fori(0, 2 * G) as c:
                load_chunk(c * PC + N_Q, N_Q, w_in_b[0], c)
            with sp.Fori(0, G) as g:
                n = g * (2 * PC) + N_KV
                load_chunk(n, N_KV, w_kv, g)
                load_chunk(n + PC, N_KV, w_kv, g + G)
            load_out_ple_gate(1, w_out_b[0])
            with sp.Fori(0, G - 1) as c:
                sp.wait_ge(x2_ready, c + (G + 1))
                sp.dma_start(out[:, bass.ts(c, COLS)].rearrange("(t p) n -> p t n", p=P),
                             columns(res[1], c)).then_inc(out_stored, 16)
            for t in range(TT):
                sp.wait_ge(x2_ready, 2 * G + t)
                sp.dma_start(out[t * P:(t + 1) * P, (G - 1) * COLS:], columns(res[1], G - 1)[:, t]) \
                    .then_inc(out_stored, 16)
            sp.wait_ge(out_stored, 16 * (G - 1 + TT))

        @block.gpsimd
        def _(pool):
            for ap, value in ((ident[:, :], 0.0), (neg_upper_raw, -1.0), (neg_ones_raw, -1.0), (past[:, :], 1.0),
                              (not_past[:, :], 0.0), (future[:, :], 0.0), (minus_half[:, :], -0.5)):
                nc.gpsimd.memset(ap, value).then_inc(consts_done, 1)
            pool.wait_ge(consts_done, 7)
            for ap, op, fill, step, mult in ((ident[:, :], ALU.not_equal, 1.0, -1, 1),
                                             (neg_upper_raw, ALU.is_ge, 0.0, -1, 1),
                                             (past[:, :], ALU.is_gt, 0.0, 1, -1),
                                             (not_past[:, :], ALU.is_gt, NEG, 1, -1),
                                             (future[:, :], ALU.is_ge, NEG, -1, 1)):
                nc.gpsimd.affine_select(out=ap, in_=ap, compare_op=op, fill=fill, base=0,
                                        pattern=[[step, P]], channel_multiplier=mult) \
                    .then_inc(consts_done, 1)

            def load_res(layer, src):
                for c in range(G):
                    pool.dma_start(columns(res[layer], c),
                                   src[:, c * COLS:(c + 1) * COLS].rearrange("(t p) n -> p t n", p=P)) \
                        .then_inc(res_landed[c], 16)

            def load_p(layer):
                pool.dma_start(p_raw, pt[layer].rearrange("(k p) t -> p k t", p=P)).then_inc(p_landed, 16)

            def load_ln_rows(layer):
                for i, row in enumerate((gain, offset)):
                    pool.dma_start(row, ln_rows[layer, i:i + 1, :].broadcast_to((P, D))) \
                        .then_inc(ln_rows_landed, 16)

            def inverse_std(k):
                pool.wait_ge(var_done, k + 1)
                nc.gpsimd.tensor_tensor(rstd[:, :], var_eps[:, :], minus_half[:, :], ALU.pow) \
                    .then_inc(rstd_done, 1)

            def gain_and_offset(layer):
                pool.wait_ge(ln_rows_landed, 32 * (layer + 1))
                for c in range(G):
                    x1 = columns(res[layer], c)
                    row = lambda r: r[:, c * COLS:(c + 1) * COLS].unsqueeze(1).broadcast_to((P, TT, COLS))
                    pool.wait_ge(lnT_psum, (2 * G if layer else 0) + c + 1)
                    nc.gpsimd.tensor_tensor(x1, x1, row(gain), ALU.mult).then_inc(gained, 1)
                    pool.wait_ge(gained, layer * G + c + 1)
                    nc.gpsimd.tensor_tensor(x1, x1, row(offset), ALU.add).then_inc(x1_ready, 1)

            pool.wait_ge(act_ready, PC)
            pool.wait_ge(masks_done, 1)
            pool.wait_ge(piece_used, 1)
            load_p(0)
            pool.dma_start(cos_sin[:, :, :, :], rope).then_inc(tables_landed, 16)
            pool.dma_start(ln_col[:, :, :, :], ln_cols).then_inc(tables_landed, 16)
            pool.wait_ge(pv_done, 2 * G)
            load_res(0, x)
            pool.wait_ge(act_ready, S_OUT[0] + G)
            load_ln_rows(0)
            inverse_std(0)
            gain_and_offset(0)
            with pool.Fori(0, G) as c:
                pool.wait_ge(x2_ready, c + 1)
                pool.dma_start(x2_spill[:, bass.ts(c, COLS)].rearrange("(t p) n -> p t n", p=P),
                               columns(res[0], c)).then_inc(x2_spilled, 16)
            inverse_std(1)
            with pool.Fori(0, G) as g:
                pool.wait_ge(qT_ready, g + (G + 1))
                pool.wait_ge(scores_ready, g * 2 + 2 * G)
                nc.gpsimd.tensor_copy(qT[:, :, 0:P], quarter(q_all, g)[:, :, 0:P]).then_inc(q_group_ready, 1)
            pool.wait_ge(q_group_ready, G)
            pool.wait_ge(q_lo, 2 * G)
            pool.wait_ge(x2_spilled, 16 * G)
            load_res(1, x2_spill)
            pool.wait_ge(pv_done, 4 * G)
            load_p(1)
            pool.wait_ge(act_ready, S_OUT[1] + G)
            load_ln_rows(1)
            inverse_std(2)
            gain_and_offset(1)

        @block.scalar
        def _(act):
            def split(n, r):
                act.wait_ge(w_landed[r % RAWS], n * 4 + (16 - 4 * (r % RAWS)))
                if not isinstance(n, int) or n >= SPLITS:
                    act.wait_ge(piece_used, n - SPLITS + 1)
                nc.scalar.activation(w_hi[:, r], raw[:, r % RAWS], ACT.Copy).then_inc(hi_ready, 1)

            def pieces(n, base, after=None, count=PC, before=None):
                for j in range(count):
                    for step in (before or {}).get(j, ()):
                        step()
                    if not isinstance(n, int) or n + j + SPLITS < PIECES:
                        split(n + (j + SPLITS), (base + j) % SPLITS)
                    for step in (after or {}).get(j, ()):
                        step()

            def operand_hi(dst, src, c):
                nc.scalar.activation(quarter(dst[:, 0], c), src, ACT.Copy).then_inc(act_hi, 1)

            def copy_qT(k, dst):
                act.wait_ge(qT_psum, k + 1)
                nc.scalar.activation(dst, aux_kt[0], ACT.Copy, scale=SCALE).then_inc(qT_ready, 1)

            def q_copies(k):
                act.wait_ge(qT_psum, k + 1)
                nc.scalar.activation(qT[:, :, P:T], aux_kt[0][:, :, P:T], ACT.Copy, scale=SCALE).then_inc(qT_ready, 1)
                nc.scalar.activation(q_parts[:, 0], aux_kt[0], ACT.Copy, scale=SCALE).then_inc(q_hi, 1)

            def k_copies(k):
                act.wait_ge(kT_psum, k + 1)
                nc.scalar.activation(kT[:, :, P:T], aux_kt[1][:, :, P:T], ACT.Copy).then_inc(kT_ready, 1)
                nc.scalar.activation(k_parts[:, 0], aux_kt[1][:, :, 0:P], ACT.Copy).then_inc(k_hi, 1)

            def values_hi(k):
                act.wait_ge(piece_used, k * (4 * PC) + 3 * PC)
                nc.scalar.activation(v_parts[:, 0], acc_of(0)[:, 0], ACT.Copy).then_inc(v_hi, 1)

            def stick_weights_hi(k, b):
                act.wait_ge(w_ready, k * 2 + (b + 1))
                act.wait_ge(cum_ready, k * 2 + 2)
                nc.scalar.activation(w_parts[:, 0, b], prob[:, b, :, 0:T], ACT.Copy).then_inc(weights_hi, 1)

            def k_copies_b(k):
                act.wait_ge(kT_psum, k + 1)
                nc.scalar.activation(kT[:, :, 0:P], aux_kt[1][:, :, 0:P], ACT.Copy).then_inc(kT_ready, 1)
                nc.scalar.activation(k1_parts[:, 0], aux_kt[1], ACT.Copy).then_inc(k_hi, 1)

            def queries_hi_b(k):
                nc.scalar.activation(q1_parts[:, 0], quarter(q_all, k - G)[:, :, P:T], ACT.Copy).then_inc(q_hi, 1)

            def values_hi_b(k, n_end):
                act.wait_ge(piece_used, n_end)
                act.wait_ge(scores_ready, k * 2 + 2)
                nc.scalar.activation(v1_parts[:, 0], acc_of(1)[:, 0], ACT.Copy).then_inc(v_hi, 1)

            def exp_abs(k, b):
                act.wait_ge(scores_ready, k * 2 + (b + 1))
                nc.scalar.activation(prob[:, b], scores_of(b), ACT.Abs).then_inc(abs_done, 1)
                act.wait_ge(abs_done, k * 2 + (b + 1))
                nc.scalar.activation(prob[:, b], prob[:, b], ACT.Exp, scale=-1.0).then_inc(exp_done, 1)

            def log_1p(k):
                for b in range(2):
                    act.wait_ge(exp_done, k * 2 + (b + 1))
                    nc.scalar.activation(prob[:, b], prob[:, b], ACT.Ln, bias=1.0).then_inc(ln_done, 1)

            def softplus_hi(k, b):
                act.wait_ge(sp_ready, k * 2 + (b + 1))
                nc.scalar.activation(sp_parts[:, 0, b], prob[:, b], ACT.Copy).then_inc(sp_hi, 1)

            def stick_weights(k, b):
                act.wait_ge(masked, k * 2 + (b + 1))
                nc.scalar.activation(prob[:, b], scores_of(b), ACT.Exp).then_inc(w_ready, 1)

            def silu_z(k, dst, src):
                act.wait_ge(zT_psum, k + 1)
                nc.scalar.activation(dst, src, ACT.Silu).then_inc(sz_ready, 1)

            def gated_hi(k, c):
                act.wait_ge(gated, k + 1)
                operand_hi(act1, gt, c)

            def silu_z_group(k):
                act.wait_ge(act_ready, k + S_OUT[0])
                silu_z(k, gt, aux[:, :].rearrange("p (b s n) -> p b s n", b=2, s=2)[:, :, 1])

            def softmax_exp(k, b):
                act.wait_ge(neg_max_ready, (k - G) * 2 + (b + 1))
                for t in range(TT):
                    for h in range(2):
                        lo, hi = (0, P) if t == 0 else (P, SC)
                        i = 2 * t + h
                        last = nc.scalar.activation(prob[:, b, h, lo:hi], aux_b[:, 2 * b + h, lo:hi], ACT.Exp,
                                                    bias=neg_max[:, b, i:i + 1],
                                                    accum_out=row_sum[:, b, i:i + 1])
                last.then_inc(probs_raw, 1)

            def probsT_copies(k, b):
                act.wait_ge(probsT_psum, (k - G) * 2 + (b + 1))
                s = scores_of(b)
                nc.scalar.activation(prob[:, b, :, T:SC], s[:, :, T:SC], ACT.Copy).then_inc(w_ready, 1)
                nc.scalar.activation(w1_parts[:, 0, b], s[:, :, 0:T], ACT.Copy).then_inc(weights_hi, 1)

            for j in range(PC):
                act.wait_ge(x_landed[j], 16)
                part = slice(PIECE_K * j, PIECE_K * (j + 1))
                nc.scalar.activation(act0[:, 0, part], x_raw[:, part], ACT.Copy).then_inc(act_hi, 1)
                split(j, j)

            act.wait_ge(consts_done, 12)
            nc.scalar.activation(neg_upper[:, :], neg_upper_raw, ACT.Copy)
            nc.scalar.activation(neg_ones[:, :], neg_ones_raw, ACT.Copy).then_inc(masks_done, 1)

            def after_k(k):
                return {4: [lambda: q_copies(k)]}

            def after_v(k):
                return {2: [lambda: k_copies(k)], 4: [lambda: exp_abs(k, 0)],
                        5: [lambda: exp_abs(k, 1), lambda: log_1p(k)],
                        6: [lambda: softplus_hi(k, 0)], 7: [lambda: softplus_hi(k, 1), lambda: values_hi(k)]}

            def after_z(k):
                return {3: [lambda: stick_weights(k, 0)],
                        4: [lambda: stick_weights(k, 1), lambda: stick_weights_hi(k, 0)],
                        5: [lambda: stick_weights_hi(k, 1)]}

            def gate_group(k):
                return {2: [lambda: silu_z_group(k)], 3: [lambda: gated_hi(k, k)]}

            pieces(0, 0)
            pieces(PC, 0, after_k(0))
            with act.Fori(0, G - 1) as g:
                n = g * (4 * PC) + 2 * PC
                pieces(n, 0, after_v(g))
                pieces(n + PC, 0, after_z(g))
                pieces(n + 2 * PC, 0, gate_group(g))
                pieces(n + 3 * PC, 0, after_k(g + 1))
            pieces(N_OUT[0] - 2 * PC, 0, after_v(G - 1))
            pieces(N_OUT[0] - PC, 0, after_z(G - 1))

            def split_p(layer):
                act.wait_ge(p_landed, 16 * (layer + 1))
                act.wait_ge(piece_used, N_OUT[layer])
                nc.scalar.activation(p_act[:, 0], p_raw, ACT.Copy).then_inc(p_hi, 1)

            def ple_out(layer, c):
                act.wait_ge(piece_used, N_PLE[layer] + c + 1)
                src = (aux if c < 2 else acc)[:, (c % 2) * 2 * COLS:(c % 2 + 1) * 2 * COLS]
                nc.scalar.activation(columns(ple[layer], c), src.rearrange(tokens, t=TT), ACT.Copy) \
                    .then_inc(ple_evac, 1)

            def normalise(k, src, dst):
                act.wait_ge(shift_done, k + 1)
                nc.scalar.activation(dst[:, 1], src[:, 1], ACT.Identity, bias=shift[:, 1:2],
                                     scale=rstd[:, 1:2]).then_inc(normed_1, 1)

            def full_hi(k, c):
                act.wait_ge(full_ready, k + 1)
                operand_hi(act0, stage_kt, c)

            def sigmoid_gate(layer, c, parity):
                act.wait_ge(piece_used, c * PC + (N_GATE[layer] + PC))
                if not isinstance(c, int) or c + layer > 0:
                    act.wait_ge(x2_ready, c + layer * G)
                if layer == 0 and not isinstance(c, int):
                    act.wait_ge(x2T_psum, c)
                nc.scalar.activation(stage_tn, acc_of(parity), ACT.Sigmoid).then_inc(sig_ready, 1)

            def x2_hi(c):
                act.wait_ge(x2T_psum, c + 1)
                operand_hi(act1, aux_kt[0], c)

            def out_ple_gate(layer, after_out):
                n = N_OUT[layer]
                pieces(n, n, after_out | {12: [lambda: split_p(layer)]}, G * PC)
                n = N_PLE[layer]
                k = 2 * G * layer
                x1 = [columns(res[layer], c) for c in range(G)]
                ple_step, full_step = ([lambda c=c: ple_out(layer, c) for c in range(G)],
                                       [lambda c=c: full_hi(k + c, c) for c in range(G)])
                pieces(n, n, count=G, before={
                    0: ple_step[0:1] + [lambda r=r: normalise(2 * layer, r, r) for r in x1]
                    + ple_step[1:2] + full_step[0:1] + ple_step[2:3] + full_step[1:2] + ple_step[3:4],
                    2: full_step[2:3]})
                n = N_GATE[layer]
                pieces(n, n, {PC - 1: [lambda: sigmoid_gate(layer, 0, 0)]}, before={0: full_step[3:4]})
                with act.Fori(1, G - layer) as c:
                    pieces(c * PC + n, n, ({3: [lambda: x2_hi(c - 1)]} if layer == 0 else {})
                           | {PC - 1: [lambda: sigmoid_gate(layer, c, c % 2)]})
                if layer:
                    for t in range(TT):
                        act.wait_ge(*((tile_0_done, LAYERS + 1) if t == 0 else (piece_used, PIECES)))
                        act.wait_ge(x2_ready, 2 * G - 1)
                        nc.scalar.activation(stage_tn[:, t], acc_of((G - 1) % 2)[:, t], ACT.Sigmoid) \
                            .then_inc(sig_ready, 1)

            out_ple_gate(0, gate_group(G - 1))

            def ln_hi(c):
                full_hi(c + G, c)

            def normalise_x2(c):
                normalise(1, columns(res[0], c), v_or_z)

            pieces(N_Q, N_Q, {2: [lambda: x2_hi(G - 1)], 3: [lambda: normalise_x2(0)], 6: [lambda: ln_hi(0)]})
            with act.Fori(1, G) as c:
                pieces(c * PC + N_Q, N_Q, {2: [lambda: copy_qT(c + (G - 1), quarter(q_all, c - 1))],
                                           3: [lambda: normalise_x2(c)], 5: [lambda: ln_hi(c)]})
            pieces(N_Z, N_Z, {2: [lambda: copy_qT(2 * G - 1, quarter(q_all, G - 1))]})
            act.wait_ge(x2_spilled, 16 * G)
            with act.Fori(1, G) as c:
                pieces(c * PC + N_Z, N_Z,
                       {2: [lambda: silu_z(c + (G - 1), quarter(sz_all, c - 1), aux_kt[0])]})
            act.wait_ge(act_ready, S_KV + G)
            pieces(N_KV, N_KV, {2: [lambda: silu_z(2 * G - 1, quarter(sz_all, G - 1), aux_kt[0])],
                                5: [lambda: queries_hi_b(G)]})

            def after_v_b(k, n):
                return {2: [lambda: k_copies_b(k)], 4: [lambda: softmax_exp(k, 0)],
                        5: [lambda: softmax_exp(k, 1)], 7: [lambda: values_hi_b(k, n + PC)]}

            def after_k_b(k):
                return {0: [lambda: probsT_copies(k, 0)], 1: [lambda: probsT_copies(k, 1)],
                        4: [lambda: gated_hi(k, k - G)]}

            with act.Fori(0, G - 1) as g:
                n = g * (2 * PC) + (N_KV + PC)
                pieces(n, N_KV, after_v_b(g + G, n))
                pieces(n + PC, N_KV, after_k_b(g + G) | {5: [lambda: queries_hi_b(g + (G + 1))]})
            pieces(N_OUT[1] - PC, N_KV, after_v_b(2 * G - 1, N_OUT[1] - PC))
            out_ple_gate(1, after_k_b(2 * G - 1))

        @block.vector
        def _(dve):
            def split(n, r):
                dve.wait_ge(hi_ready, n + 1)
                nc.vector.tensor_tensor(w_lo[:, r], raw[:, r % RAWS], w_hi[:, r].bitcast(F32), ALU.subtract) \
                    .then_inc(lo_ready, 1)

            def pieces(n, base, after=None, count=PC, before=None):
                for j in range(count):
                    for step in (before or {}).get(j, ()):
                        step()
                    if not isinstance(n, int) or n + j + SPLITS < PIECES:
                        split(n + (j + SPLITS), (base + j) % SPLITS)
                    for step in (after or {}).get(j, ()):
                        step()

            def operand_lo(s, dst, src, c):
                dve.wait_ge(act_hi, s + 1)
                nc.vector.tensor_tensor(quarter(dst[:, 1], c), src, quarter(dst[:, 0], c).bitcast(F32),
                                        ALU.subtract).then_inc(act_ready, 1)

            def evacuate(n_end, parity, dst):
                dve.wait_ge(piece_used, n_end)
                nc.vector.tensor_scalar(dst, acc_of(parity), 1.0, None, ALU.mult).then_inc(chunk_evac, 1)

            def softplus(k, b):
                dve.wait_ge(ln_done, k * 2 + (b + 1))
                nc.vector.scalar_tensor_tensor(out=prob[:, b], in0=scores_of(b), scalar=0.0, in1=prob[:, b],
                                               op0=ALU.max, op1=ALU.add).then_inc(sp_raw, 1)
                dve.wait_ge(sp_raw, k * 2 + (b + 1))
                for h in range(2):
                    diagonal = prob[:, b, h].rearrange("p (s c) -> p s c", c=P)[:, 0:3:2]
                    last = nc.vector.tensor_tensor(diagonal, diagonal,
                                                   past[:, :].unsqueeze(1).broadcast_to((P, 2, P)), ALU.mult)
                last.then_inc(sp_ready, 1)

            def mask_scores(k, b, mask):
                blocks = scores_of(b).rearrange("p h (s c) -> p h s c", c=P)[:, :, 0:3:2]
                nc.vector.tensor_tensor(blocks, blocks, mask[:, :].unsqueeze(1).unsqueeze(1).broadcast_to((P, 2, 2, P)),
                                        ALU.add).then_inc(masked, 1)

            def mask_stick(k, b):
                dve.wait_ge(cum_ready, k * 2 + (b + 1))
                mask_scores(k, b, not_past)

            def queries_lo(k):
                dve.wait_ge(q_hi, k + 1)
                nc.vector.scalar_tensor_tensor(out=q_parts[:, 1], in0=aux_kt[0], scalar=SCALE,
                                               in1=q_parts[:, 0].bitcast(F32), op0=ALU.mult, op1=ALU.subtract) \
                    .then_inc(q_lo, 1)

            def keys_lo(k):
                dve.wait_ge(k_hi, k + 1)
                nc.vector.tensor_tensor(k_parts[:, 1], aux_kt[1][:, :, 0:P], k_parts[:, 0].bitcast(F32),
                                        ALU.subtract).then_inc(k_lo, 1)

            def values_lo(k):
                dve.wait_ge(v_hi, k + 1)
                nc.vector.tensor_tensor(v_parts[:, 1], acc_of(0)[:, 0], v_parts[:, 0].bitcast(F32),
                                        ALU.subtract).then_inc(v_lo, 1)

            def stick_weights_lo(k, b):
                dve.wait_ge(weights_hi, k * 2 + (b + 1))
                nc.vector.tensor_tensor(w_parts[:, 1, b], prob[:, b, :, 0:T], w_parts[:, 0, b].bitcast(F32),
                                        ALU.subtract).then_inc(weights_lo, 1)

            def softplus_lo(k, b):
                dve.wait_ge(sp_hi, k * 2 + (b + 1))
                nc.vector.tensor_tensor(sp_parts[:, 1, b], prob[:, b], sp_parts[:, 0, b].bitcast(F32),
                                        ALU.subtract).then_inc(sp_lo, 1)

            def gate_group(k, c, sz):
                dve.wait_ge(sz_ready, k + 1)
                dve.wait_ge(pv_done, k * 2 + 2)
                o = aux[:, :].rearrange("p (b s n) -> p b s n", b=2, s=2)[:, :, 0]
                nc.vector.tensor_tensor(gt.rearrange("p (b h) t -> p b (h t)", b=2), o,
                                        sz.rearrange("p (b h) t -> p b (h t)", b=2), ALU.mult).then_inc(gated, 1)

            def gated_lo(k, c, s):
                operand_lo(s, act1, gt, c)

            for j in range(PC):
                dve.wait_ge(act_hi, j + 1)
                part = slice(PIECE_K * j, PIECE_K * (j + 1))
                nc.vector.tensor_tensor(act0[:, 1, part], x_raw[:, part], act0[:, 0, part].bitcast(F32),
                                        ALU.subtract).then_inc(act_ready, 1)
                split(j, j)

            def chunk_end(n, parity, dst):
                return {PC - 1: [lambda: evacuate(n + PC, parity, dst)]}

            def k_steps(k, n):
                return {4: [lambda: queries_lo(k)]} | chunk_end(n, 1, kn)

            def v_steps(k, n):
                return {2: [lambda: keys_lo(k)], 5: [lambda: softplus(k, 0)], 6: [lambda: softplus(k, 1)],
                        7: [lambda: softplus_lo(k, 0), lambda: values_lo(k), lambda: evacuate_v(n, 0, vn_a)]}

            def evacuate_v(n, parity, dst):
                dve.wait_ge(piece_used, n + PC)
                nc.vector.tensor_scalar(dst[:, 1], acc_of(parity)[:, 1], 1.0, None, ALU.mult).then_inc(chunk_evac, 1)

            def z_steps(k, n):
                return {0: [lambda: softplus_lo(k, 1)], 2: [lambda: mask_stick(k, 0)], 3: [lambda: mask_stick(k, 1)],
                        4: [lambda: stick_weights_lo(k, 0)], 5: [lambda: stick_weights_lo(k, 1)]} \
                    | chunk_end(n, 1, zn_a)

            def gate_steps(k):
                return {2: [lambda: gate_group(k, k, gt)], 3: [lambda: gated_lo(k, k, k + S_OUT[0])]}

            dve.wait_ge(consts_done, 12)
            pieces(0, 0, chunk_end(0, 0, qn))
            pieces(PC, 0, k_steps(0, PC))
            with dve.Fori(0, G - 1) as g:
                n = g * (4 * PC) + 2 * PC
                pieces(n, 0, v_steps(g, n))
                pieces(n + PC, 0, z_steps(g, n + PC))
                pieces(n + 2 * PC, 0, gate_steps(g) | chunk_end(n + 2 * PC, 0, qn))
                pieces(n + 3 * PC, 0, k_steps(g + 1, n + 3 * PC))
            n = N_OUT[0] - 2 * PC
            pieces(n, 0, v_steps(G - 1, n))
            pieces(n + PC, 0, z_steps(G - 1, n + PC))

            def add_residual(layer, c, used):
                dve.wait_ge(piece_used, N_OUT[layer] + used)
                dve.wait_ge(res_landed[c], 16 * (layer + 1))
                r = columns(res[layer], c)
                nc.vector.scalar_tensor_tensor(out=r, in0=r, scalar=ALPHA, in1=acc_of(c % 2),
                                               op0=ALU.mult, op1=ALU.add).then_inc(chunk_evac, 1)
                dve.wait_ge(chunk_evac, C_OUT[layer] + c + 1)
                statistics(r, c)

            def add_last_residual(layer):
                c = G - 1
                dve.wait_ge(res_landed[c], 16 * (layer + 1))
                r = columns(res[layer], c)
                for t, (done, count, added) in enumerate((
                        (tile_0_done, layer + 1, tile_0_added),
                        (piece_used, N_PLE[layer], chunk_evac))):
                    dve.wait_ge(done, count)
                    nc.vector.scalar_tensor_tensor(out=r[:, t], in0=r[:, t], scalar=ALPHA, in1=acc_of(c % 2)[:, t],
                                                   op0=ALU.mult, op1=ALU.add).then_inc(added, 1)
                    dve.wait_ge(added, layer + 1 if t == 0 else C_OUT[layer] + G)
                    stat = nc.vector.bn_stats(stats[:, t, c, :], r[:, t])
                stat.then_inc(stats_done, 1)

            def statistics(r, c):
                for t in range(TT):
                    s = stats[:, t, c, :] if isinstance(c, int) else stats[:, t, bass.ds(c, 1), :]
                    last = nc.vector.bn_stats(s, r[:, t])
                last.then_inc(stats_done, 1)

            def find_shift(k):
                dve.wait_ge(stats_done, G * (k + 1))
                for t in range(TT):
                    last = nc.vector.bn_aggr(moments[:, t], stats[:, t])
                last.then_inc(moments_done, 1)
                dve.wait_ge(moments_done, k + 1)
                nc.vector.tensor_scalar(var_eps[:, :], moments[:, :, 1], LN_EPS, None, ALU.add).then_inc(var_done, 1)
                dve.wait_ge(rstd_done, k + 1)
                nc.vector.scalar_tensor_tensor(out=shift[:, :], in0=moments[:, :, 0], scalar=-1.0, in1=rstd[:, :],
                                               op0=ALU.mult, op1=ALU.mult).then_inc(shift_done, 1)
                dve.wait_ge(shift_done, k + 1)

            def normalise(src, dst):
                nc.vector.tensor_scalar(dst[:, 0], src[:, 0], rstd[:, 0:1], shift[:, 0:1],
                                        ALU.mult, ALU.add).then_inc(normed_0, 1)

            def full_quarter(k, c, pair, which, s):
                dve.wait_ge(lnT_psum, k + 1)
                dve.wait_ge(act_ready, s)
                for i in range(HG):
                    if isinstance(c, int):
                        g, b = (ln_col[:, which, s, HG * c + i:HG * c + i + 1] for s in range(2))
                    else:
                        g, b = (ln_col[:, which, s, bass.ds(c * HG + i, 1)] for s in range(2))
                    last = nc.vector.tensor_scalar(stage_kt[:, i], aux_kt[pair][:, i], g, b, ALU.mult, ALU.add)
                last.then_inc(full_ready, 1)

            def full_lo(s, c):
                operand_lo(s, act0, stage_kt, c)

            def split_p(layer):
                dve.wait_ge(p_hi, layer + 1)
                nc.vector.tensor_tensor(p_act[:, 1], p_raw, p_act[:, 0].bitcast(F32), ALU.subtract) \
                    .then_inc(p_ready, 1)

            def add_ple(layer, c):
                e = c + layer * G
                r = columns(res[layer], c)
                dve.wait_ge(sig_ready, e + 1)
                dve.wait_ge(ple_evac, G * (layer + 1))
                nc.vector.tensor_tensor(stage_tn, stage_tn, columns(ple[layer], c), ALU.mult).then_inc(chunk_evac, 1)
                dve.wait_ge(chunk_evac, c + (C_GATE[layer] + 1))
                dve.wait_ge(x1_ready, e + 1)
                if layer:
                    nc.vector.tensor_tensor(r, r, stage_tn, ALU.add).then_inc(x2_ready, 1)
                else:
                    nc.vector.tensor_tensor(stage_tn, r, stage_tn, ALU.add).then_inc(x2_sum, 1)
                    dve.wait_ge(x2_sum, e + 1)
                    nc.vector.tensor_scalar(r, stage_tn, 1.0, None, ALU.mult).then_inc(x2_ready, 1)
                    statistics(stage_tn, c)

            def x2_lo(c):
                operand_lo(c + S_X2, act1, aux_kt[0], c)

            def out_ple_gate(layer, after_out):
                n = N_OUT[layer]
                s = S_GATE[layer]
                k = 2 * G * layer
                ends = {OUT_ORDER.index((c, PC - 1)): c for c in range(G)}
                x1 = [columns(res[layer], c) for c in range(G)]
                turned = [[lambda c=c: full_quarter(k + c, c, c % 2, layer, s + c), lambda c=c: full_lo(s + c, c)]
                          for c in range(G)]
                pieces(n, n, after_out | {12: [lambda: split_p(layer)]}, G * PC,
                       before={i: [lambda c=c, i=i: add_residual(layer, c, i + 1)] for i, c in ends.items()
                               if c < G - 1}
                       | {G * PC - 1: [lambda: add_last_residual(layer), lambda: find_shift(2 * layer)]
                          + [lambda r=r: normalise(r, r) for r in x1] + turned[0]})
                pieces(N_PLE[layer], N_PLE[layer], count=G,
                       before={0: turned[1], 2: turned[2]})
                n = N_GATE[layer]
                pieces(n, n, {PC - 1: [lambda: add_ple(layer, 0)]}, before={0: turned[3]})
                with dve.Fori(1, G - layer) as c:
                    pieces(c * PC + n, n, ({3: [lambda: x2_lo(c - 1)]} if layer == 0 else {})
                           | {PC - 1: [lambda: add_ple(layer, c)]})
                if layer:
                    c = G - 1
                    dve.wait_ge(ple_evac, 2 * G)
                    dve.wait_ge(x1_ready, 2 * G)
                    for t in range(TT):
                        r, gate = columns(res[1], c)[:, t], stage_tn[:, t]
                        dve.wait_ge(sig_ready, 2 * G + t)
                        nc.vector.tensor_tensor(gate, gate, columns(ple[1], c)[:, t], ALU.mult) \
                            .then_inc(chunk_evac, 1)
                        dve.wait_ge(chunk_evac, C_GATE[1] + G + t)
                        nc.vector.tensor_tensor(r, r, gate, ALU.add).then_inc(x2_ready, 1)

            out_ple_gate(0, gate_steps(G - 1))

            def rotate(n_end, parity):
                dve.wait_ge(piece_used, n_end)
                src = acc_of(parity).rearrange("p t (h d) -> p t h d", d=DH)
                first, second = src[:, :, :, 0:HALF], src[:, :, :, HALF:DH]
                cos, sin = (cos_sin[:, i].unsqueeze(2).broadcast_to((P, TT, HG, HALF)) for i in range(2))
                nc.vector.tensor_tensor(roped_out[:, :, :, 0:HALF], first, cos, ALU.mult)
                nc.vector.tensor_tensor(roped_out[:, :, :, HALF:DH], second, cos, ALU.mult)
                nc.vector.tensor_tensor(rope_tmp[:, :, :, 0:HALF], second, sin, ALU.mult).then_inc(rope_mul, 1)
                nc.vector.tensor_tensor(rope_tmp[:, :, :, HALF:DH], first, sin, ALU.mult).then_inc(chunk_evac, 1)

            def rotate_end(k, c_evac):
                dve.wait_ge(rope_mul, k + 1)
                dve.wait_ge(chunk_evac, c_evac)
                nc.vector.tensor_tensor(roped_out[:, :, :, 0:HALF], roped_out[:, :, :, 0:HALF],
                                        rope_tmp[:, :, :, 0:HALF], ALU.subtract)
                nc.vector.tensor_tensor(roped_out[:, :, :, HALF:DH], roped_out[:, :, :, HALF:DH],
                                        rope_tmp[:, :, :, HALF:DH], ALU.add).then_inc(roped, 1)

            def q_end(c, parity):
                return {PC - 1: [lambda: rotate(c * PC + (N_Q + PC), parity),
                                 lambda: rotate_end(c, c + (C_Q + 1))]}

            def normalise_x2(c):
                normalise(columns(res[0], c), v_or_z)

            def ln_quarter(c):
                return [lambda: full_quarter(c + G, c, 1, 2, c + S_KV), lambda: full_lo(c + S_KV, c)]

            dve.wait_ge(tables_landed, 32)
            pieces(N_Q, N_Q, {2: [lambda: x2_lo(G - 1), lambda: find_shift(1), lambda: normalise_x2(0)],
                               6: ln_quarter(0)} | q_end(0, 0))
            with dve.Fori(1, G) as c:
                pieces(c * PC + N_Q, N_Q, {3: [lambda: normalise_x2(c)], 5: ln_quarter(c)} | q_end(c, c % 2))
            pieces(N_Z, N_Z, chunk_end(N_Z, 0, v_or_z[:, :, :]))
            with dve.Fori(1, G) as c:
                n = c * PC + N_Z
                pieces(n, N_Z, chunk_end(n, c % 2, v_or_z[:, :, :]))

            def k_end(n, g):
                return {PC - 1: [lambda: rotate(n + PC, 0),
                                 lambda: rotate_end(g + G, g * 2 + (C_KV + 1))]}

            def row_max(k, b):
                dve.wait_ge(scores_ready, k * 2 + (b + 1))
                mask_scores(k, b, future)
                dve.wait_ge(masked, k * 2 + (b + 1))
                for t, (lo, hi) in enumerate(((0, P), (P, SC))):
                    last = nc.vector.tensor_reduce(out=neg_max[:, b, 2 * t:2 * t + 2],
                                                   in_=aux_b[:, 2 * b:2 * b + 2, lo:hi],
                                                   axis=AX.X, op=ALU.max, negate=True)
                last.then_inc(neg_max_ready, 1)

            def divide(k, b):
                i = (k - G) * 2 + (b + 1)
                dve.wait_ge(probs_raw, i)
                nc.vector.reciprocal(row_sum[:, b], row_sum[:, b]).then_inc(inv_ready, 1)
                dve.wait_ge(inv_ready, i)
                for t, (lo, hi) in enumerate(((0, P), (P, SC))):
                    part = prob[:, b, :, lo:hi]
                    last = nc.vector.tensor_tensor(
                        part, part, row_sum[:, b, 2 * t:2 * t + 2].unsqueeze(2).broadcast_to((P, 2, hi - lo)),
                        ALU.mult)
                last.then_inc(probs_ready, 1)

            def queries_lo_b(k):
                dve.wait_ge(q_hi, k + 1)
                nc.vector.tensor_tensor(q1_parts[:, 1], quarter(q_all, k - G)[:, :, P:T],
                                        q1_parts[:, 0].bitcast(F32), ALU.subtract).then_inc(q_lo, 1)

            def keys_lo_b(k):
                dve.wait_ge(k_hi, k + 1)
                nc.vector.tensor_tensor(k1_parts[:, 1], aux_kt[1], k1_parts[:, 0].bitcast(F32),
                                        ALU.subtract).then_inc(k_lo, 1)

            def values_lo_b(k):
                dve.wait_ge(v_hi, k + 1)
                nc.vector.tensor_tensor(v1_parts[:, 1], acc_of(1)[:, 0], v1_parts[:, 0].bitcast(F32),
                                        ALU.subtract).then_inc(v_lo, 1)

            def probs_lo(k, b):
                dve.wait_ge(weights_hi, k * 2 + (b + 1))
                nc.vector.tensor_tensor(w1_parts[:, 1, b], scores_of(b)[:, :, 0:T], w1_parts[:, 0, b].bitcast(F32),
                                        ALU.subtract).then_inc(weights_lo, 1)

            def after_v_b(k, n):
                return {2: [lambda: keys_lo_b(k)],
                        4: [lambda: row_max(k, 0)], 5: [lambda: row_max(k, 1), lambda: divide(k, 0)],
                        6: [lambda: divide(k, 1)],
                        7: [lambda: values_lo_b(k), lambda: evacuate_v(n, 1, v_or_z)]}

            def after_k_b(k):
                return {0: [lambda: probs_lo(k, 0)], 1: [lambda: probs_lo(k, 1)],
                        4: [lambda: gate_group(k, k - G, quarter(sz_all, k - G)),
                            lambda: gated_lo(k, k - G, (k - G) + S_OUT[1])]}

            pieces(N_KV, N_KV, {5: [lambda: queries_lo_b(G)]} | k_end(N_KV, 0))
            with dve.Fori(0, G - 1) as g:
                n = g * (2 * PC) + (N_KV + PC)
                pieces(n, N_KV, after_v_b(g + G, n))
                pieces(n + PC, N_KV, after_k_b(g + G) | {5: [lambda: queries_lo_b(g + (G + 1))]}
                       | k_end(n + PC, g + 1))
            n = N_OUT[1] - PC
            pieces(n, N_KV, after_v_b(2 * G - 1, n))
            out_ple_gate(1, after_k_b(2 * G - 1))

        @block.tensor
        def _(pe):
            def piece(n, r, operand, tiles, out_banks, first, final, by_token=False):
                pe.wait_ge(lo_ready, n + 1)
                order = [(i, t) for i in range(PIECE_K) for t in range(TT)]
                for i, t in sorted(order, key=lambda it: it[1]) if by_token else order:
                    hi, lo = (operand[:, s, tiles[i], t * P:(t + 1) * P] for s in range(2))
                    dst = out_banks[:, t]
                    begin, end = first and i == 0, final and i == PIECE_K - 1
                    nc.tensor.matmul(dst, hi, w_hi[:, r, i], start=begin, stop=False)
                    nc.tensor.matmul(dst, hi, w_lo[:, r, i], start=False, stop=False)
                    mm = nc.tensor.matmul(dst, lo, w_hi[:, r, i], start=False, stop=end)
                    if by_token and t == 0 and end:
                        mm.then_inc(tile_0_done, 1)
                mm.then_inc(piece_used, 1)

            def chunk(n, base, operand, parity, c, quarters=None, after=None, last=False):
                if not isinstance(c, int) or c >= 2:
                    pe.wait_ge(chunk_evac, c - 1)
                for j in range(PC):
                    if quarters == S_X:
                        pe.wait_ge(act_ready, j + 1)
                    elif quarters is not None and j % 2 == 0:
                        pe.wait_ge(act_ready, quarters + j // 2 + 1)
                    piece(n + j, (base + j) % SPLITS, operand, range(PIECE_K * j, PIECE_K * (j + 1)),
                          acc_of(parity), j == 0, j == PC - 1, by_token=last and j == PC - 1)
                    for step in (after or {}).get(j, ()):
                        step()

            def transposes(src, dst, signal):
                for i in range(HG):
                    for t in range(TT):
                        mm = nc.tensor.transpose(dst[:, i, t * P:(t + 1) * P], src[:, t, i * P:(i + 1) * P],
                                                 ident[:, :])
                mm.then_inc(signal, 1)

            def q_turn(k, c):
                pe.wait_ge(chunk_evac, c + 1)
                if not isinstance(k, int) or k > 0:
                    pe.wait_ge(gated, k)
                transposes(qn, aux_kt[0], qT_psum)

            def k_turn(k, c):
                pe.wait_ge(chunk_evac, c + 1)
                transposes(kn, aux_kt[1], kT_psum)

            def three_passes(dst, lhs, rhs, start):
                for i, (a, b) in enumerate(((0, 0), (0, 1), (1, 0))):
                    mm = nc.tensor.matmul(dst, lhs(a), rhs(b), start=start and i == 0, stop=True,
                                          skip_group_check=True)
                return mm

            def key_scores(k, b):
                pe.wait_ge(qT_ready, k + 1)
                pe.wait_ge(kT_ready, k + 1)
                pe.wait_ge(q_lo, k + 1)
                pe.wait_ge(k_lo, k + 1)
                for h in (2 * b, 2 * b + 1):
                    s = aux_b[:, h]
                    three_passes(s[:, 0:T], lambda i, h=h: k_parts[:, i, h], lambda i, h=h: q_parts[:, i, h], True)
                    mm = nc.tensor.matmul(s[:, T:SC], kT[:, h, P:T], qT[:, h, P:T], start=False, stop=True,
                                          skip_group_check=True)
                mm.then_inc(scores_ready, 1)

            def cumulate(k, b):
                pe.wait_ge(sp_lo, k * 2 + (b + 1))
                for i, h in enumerate((2 * b, 2 * b + 1)):
                    s, (hi, lo) = aux_b[:, h], (sp_parts[:, part, b, i] for part in range(2))
                    for dst, lhs, rhs in ((s[:, 0:SC], neg_upper, hi), (s[:, 0:SC], neg_upper, lo),
                                          (s[:, P:T], neg_ones, hi[:, T:SC]), (s[:, P:T], neg_ones, lo[:, T:SC])):
                        mm = nc.tensor.matmul(dst, lhs[:, :], rhs, start=False, stop=True,
                                              skip_group_check=True)
                mm.then_inc(cum_ready, 1)

            def weigh_values(k, b, v_chunk, v_parts, v, w_parts):
                pe.wait_ge(weights_lo, k * 2 + (b + 1))
                pe.wait_ge(w_ready, k * 2 + (b + 1))
                pe.wait_ge(v_lo, k + 1)
                pe.wait_ge(chunk_evac, v_chunk + 1)
                for i in range(2):
                    head = slice((2 * b + i) * P, (2 * b + i + 1) * P)
                    o = aux_b[:, 2 * b, i * T:(i + 1) * T]
                    three_passes(o, lambda part: v_parts[:, part, head], lambda part: w_parts[:, part, b, i], i == 0)
                    mm = nc.tensor.matmul(o[:, P:T], v[:, 1, head], prob[:, b, i, T:SC], start=False, stop=True,
                                          skip_group_check=True)
                mm.then_inc(pv_done, 1)

            def z_turn(k, c):
                pe.wait_ge(chunk_evac, c + 1)
                for i in range(HG):
                    for t in range(TT):
                        bank = aux_b[:, 2 * (i // 2) + 1]
                        at = (i % 2) * T + t * P
                        mm = nc.tensor.transpose(bank[:, at:at + P], zn_a[:, t, i * P:(i + 1) * P], ident[:, :])
                mm.then_inc(zT_psum, 1)

            def after_k(k, c):
                return {4: [lambda: q_turn(k, c - 1)]}

            def after_v(k, c):
                return {2: [lambda: k_turn(k, c - 1)], 4: [lambda: key_scores(k, 0)],
                        5: [lambda: key_scores(k, 1)]}

            def after_z(k, c):
                return {2: [lambda: cumulate(k, 0)], 3: [lambda: cumulate(k, 1)],
                        6: [lambda: weigh_values(k, 0, c - 1, v_parts, vn_a, w_parts)],
                        7: [lambda: weigh_values(k, 1, c - 1, v_parts, vn_a, w_parts)]}

            def z_step(k, c):
                return {2: [lambda: z_turn(k, c)]}

            pe.wait_ge(consts_done, 3)
            for _ in range(WARM_UPS):
                nc.tensor.matmul(aux[:, 0:P], neg_ones_raw, neg_ones_raw, start=True, stop=True)
            pe.wait_ge(consts_done, 12)
            chunk(0, 0, act0, 0, 0, quarters=S_X)
            chunk(PC, 0, act0, 1, 1, after=after_k(0, 1))
            pe.wait_ge(masks_done, 1)
            with pe.Fori(0, G - 1) as g:
                n = g * (4 * PC) + 2 * PC
                c = g * 4 + 2
                chunk(n, 0, act0, 0, c, after=after_v(g, c))
                chunk(n + PC, 0, act0, 1, c + 1, after=after_z(g, c + 1))
                chunk(n + 2 * PC, 0, act0, 0, c + 2, after=z_step(g, c + 1))
                chunk(n + 3 * PC, 0, act0, 1, c + 3, after=after_k(g + 1, c + 3))
            c = C_OUT[0] - 2
            chunk(c * PC, 0, act0, 0, c, after=after_v(G - 1, c))
            chunk((c + 1) * PC, 0, act0, 1, c + 1, after=after_z(G - 1, c + 1))

            def ln_turn(k, c, pair, layer, src):
                pe.wait_ge(normed_0, k + 1)
                pe.wait_ge(normed_1, k + 1)
                transposes(src if c is None else columns(src, c), aux_kt[pair], lnT_psum)

            def out_projection(layer, after_out):
                for i, (c, j) in enumerate(OUT_ORDER):
                    n = N_OUT[layer] + i
                    if j == 0:
                        pe.wait_ge(chunk_evac, C_OUT[layer] + c - 1)
                    if c == 0 and j % 2 == 0:
                        pe.wait_ge(act_ready, S_OUT[layer] + j // 2 + 1)
                    piece(n, n % SPLITS, act1, range(PIECE_K * j, PIECE_K * (j + 1)), acc_of(c % 2),
                          j == 0, j == PC - 1, by_token=i == G * PC - 1)
                    for step in after_out.get(i, ()):
                        step()

            def ple_and_gate(layer):
                k = 2 * G * layer
                s = S_GATE[layer]

                def turn(i):
                    if i < 2:
                        pe.wait_ge(ple_evac, layer * G + i + 1)
                    else:
                        pe.wait_ge(full_ready, k + i - 1)
                    ln_turn(k + i, i, i % 2, layer, res[layer])

                pe.wait_ge(p_ready, layer + 1)
                for c in range(G):
                    n = N_PLE[layer] + c
                    if c >= 2:
                        pe.wait_ge(chunk_evac, C_OUT[layer] + c + 1)
                    banks = acc_of(c % 2) if c >= 2 else \
                        aux[:, c * 2 * COLS:(c + 1) * 2 * COLS].rearrange(tokens, t=TT)
                    piece(n, n % SPLITS, act0, range(KT - PIECE_K, KT), banks, True, True)
                    if c >= 1:
                        turn(c - 1)
                n, c0 = N_GATE[layer], C_GATE[layer]
                pe.wait_ge(ple_evac, layer * G + G - 1)
                chunk(n, n, act0, 0, c0, quarters=s, after={1: [lambda: turn(3)]})
                pe.wait_ge(ple_evac, layer * G + G)
                with pe.Fori(1, G - layer) as c:
                    chunk(c * PC + n, n, act0, c % 2, c + c0,
                          after={3: [lambda: x2_turn(c - 1)]} if layer == 0 else None)
                if layer:
                    c = G - 1
                    chunk(c * PC + n, n, act0, c % 2, c + c0, last=True)

            def x2_turn(c):
                pe.wait_ge(x2_ready, c + 1)
                pe.wait_ge(act_ready, c + S_X2)
                transposes(stage_tn, aux_kt[0], x2T_psum)

            out_projection(0, z_step(G - 1, C_OUT[0] - 1))
            ple_and_gate(0)

            def ln_step(c):
                if not isinstance(c, int):
                    pe.wait_ge(full_ready, c + G)
                ln_turn(c + G, None, 1, 0, v_or_z)

            def q_turn_b(c):
                pe.wait_ge(roped, c + 1)
                if isinstance(c, int) and c == 0:
                    pe.wait_ge(act_ready, S_X2 + G)
                else:
                    pe.wait_ge(qT_ready, c + G)
                transposes(roped_rows, aux_kt[0], qT_psum)

            def z_turn_b(c):
                pe.wait_ge(chunk_evac, c + (C_Z + 1))
                pe.wait_ge(sz_ready, c + G)
                transposes(v_or_z, aux_kt[0], zT_psum)

            def k_turn_b(k):
                pe.wait_ge(roped, k + 1)
                pe.wait_ge(gated, k)
                transposes(roped_rows, aux_kt[1], kT_psum)

            def query_scores(k, b):
                pe.wait_ge(kT_ready, k + 1)
                pe.wait_ge(q_group_ready, (k - G) + 1)
                pe.wait_ge(q_lo, k + 1)
                pe.wait_ge(k_lo, k + 1)
                for h in (2 * b, 2 * b + 1):
                    s = aux_b[:, h]
                    nc.tensor.matmul(s[:, 0:P], qT[:, h, 0:P], kT[:, h, 0:P], start=True, stop=True,
                                     skip_group_check=True)
                    mm = three_passes(s[:, P:SC], lambda i, h=h: q1_parts[:, i, h],
                                      lambda i, h=h: k1_parts[:, i, h], False)
                mm.then_inc(scores_ready, 1)

            def probs_turn(k, b):
                pe.wait_ge(probs_ready, (k - G) * 2 + (b + 1))
                for i in range(2):
                    for s in range(3):
                        mm = nc.tensor.transpose(aux_b[:, 2 * b + i, s * P:(s + 1) * P],
                                                 prob[:, b, i, s * P:(s + 1) * P], ident[:, :])
                mm.then_inc(probsT_psum, 1)

            chunk(N_Q, N_Q, act1, 0, C_Q, quarters=S_X2,
                  after={2: [lambda: x2_turn(G - 1)], 6: [lambda: ln_step(0)]})
            with pe.Fori(1, G) as c:
                chunk(c * PC + N_Q, N_Q, act1, c % 2, c + C_Q,
                      after={2: [lambda: q_turn_b(c - 1)], 5: [lambda: ln_step(c)]})
            chunk(N_Z, N_Z, act1, 0, C_Z, after={2: [lambda: q_turn_b(G - 1)]})
            with pe.Fori(1, G) as c:
                chunk(c * PC + N_Z, N_Z, act1, c % 2, c + C_Z, after={2: [lambda: z_turn_b(c - 1)]})

            def after_v_b(k):
                return {2: [lambda: k_turn_b(k)], 4: [lambda: query_scores(k, 0)],
                        5: [lambda: query_scores(k, 1)]}

            def after_k_b(k, v_chunk):
                return {0: [lambda: probs_turn(k, 0)], 1: [lambda: probs_turn(k, 1)],
                        3: [lambda: weigh_values(k, 0, v_chunk, v1_parts, v_or_z, w1_parts)],
                        4: [lambda: weigh_values(k, 1, v_chunk, v1_parts, v_or_z, w1_parts)]}

            chunk(N_KV, N_KV, act0, 0, C_KV, quarters=S_KV, after={2: [lambda: z_turn_b(G - 1)]})
            pe.wait_ge(sz_ready, 2 * G)
            with pe.Fori(0, G - 1) as g:
                n = g * (2 * PC) + (N_KV + PC)
                c = g * 2 + (C_KV + 1)
                chunk(n, N_KV, act0, 1, c, after=after_v_b(g + G))
                chunk(n + PC, N_KV, act0, 0, c + 1, after=after_k_b(g + G, c))
            c = C_OUT[1] - 1
            chunk(N_OUT[1] - PC, N_KV, act0, 1, c, after=after_v_b(2 * G - 1))
            out_projection(1, after_k_b(2 * G - 1, c))
            ple_and_gate(1)


def kernel(x, p, w_in_a, w_out_a, w_kv, ln_kv_g, ln_kv_b, w_in_b, w_out_b, ln_g, ln_b, w_ple, w_ple_gate):
    import concourse.bacc as bacc
    from concourse.bass_utils import run_bass_kernel_spmd

    x, p, ln_g, ln_b, ln_kv_g, ln_kv_b = (np.asarray(a) for a in (x, p, ln_g, ln_b, ln_kv_g, ln_kv_b))
    depth, _, seq, d = p.shape[0], p.shape[1], x.shape[1], x.shape[2]
    tiles = d // P
    half = P // 2
    inv_freq = np.float32(10000.0) ** (-np.arange(half, dtype=np.float32) / np.float32(half))
    angle = np.arange(seq, dtype=np.float32)[:, None] * inv_freq[None, :]
    rope = np.stack([np.cos(angle), np.sin(angle)]).astype(np.float32)
    by_feature = np.stack([np.stack([ln_g[0], ln_b[0]]), np.stack([ln_g[1], ln_b[1]]),
                           np.stack([ln_kv_g, ln_kv_b])])
    arrays = {
        "xt": np.ascontiguousarray(x[0].T),
        "x": np.ascontiguousarray(x[0]),
        "pt": np.ascontiguousarray(p[:, 0].transpose(0, 2, 1)),
        "w_in_a": np.asarray(w_in_a), "w_out_a": np.asarray(w_out_a), "w_kv": np.asarray(w_kv),
        "w_in_b": np.asarray(w_in_b), "w_out_b": np.asarray(w_out_b), "w_ple": np.asarray(w_ple),
        "w_ple_gate": np.asarray(w_ple_gate),
        "ln_rows": np.ascontiguousarray(np.stack([ln_g, ln_b], axis=1)),
        "ln_cols": np.ascontiguousarray(by_feature.reshape(3, 2, tiles, P).transpose(3, 0, 1, 2)),
        "rope": np.ascontiguousarray(rope.reshape(2, seq // P, P, half).transpose(2, 0, 1, 3)),
    }
    assert depth == 2
    nc = bacc.Bacc("TRN2", target_bir_lowering=False, num_devices=1)
    args = [nc.dram_tensor(f"in_{n}", a.shape, mybir.dt.from_np(a.dtype), kind="ExternalInput").ap()
            for n, a in arrays.items()]
    out = nc.dram_tensor("out", (seq, d), F32, kind="ExternalOutput").ap()
    build(nc, *args, out)
    r = run_bass_kernel_spmd(nc, [{f"in_{n}": a for n, a in arrays.items()}], core_ids=[0])
    return np.asarray(r.results[0]["out"]).reshape(1, seq, d)
```
